# Optimizing a Trainium2 kernel written in Bass

```python
import math
import jax, jax.numpy as jnp
from jax import lax
import numpy as np

D_MODEL = 1024
BATCH = 1
SEQ = 256
DEPTH = 2

GRID_W = 64
CTX_LEN = 256
N_MIXERS = 3
N_POOL_LAYERS = len(range(0, DEPTH, N_MIXERS))
N_DIFF_LAYERS = len(range(1, DEPTH, N_MIXERS))
N_NAT_LAYERS = len(range(2, DEPTH, N_MIXERS))
D_FF = ((8 * D_MODEL // 3 + 255) // 256) * 256
N_MOD = 9
POOL_WINDOWS = (2, 4, 8, 16)
POOL_GROUPS = len(POOL_WINDOWS)
POOL_GW = D_MODEL // POOL_GROUPS
DIFF_HEADS = 8
DIFF_HD = D_MODEL // DIFF_HEADS // 2
NAT_HEADS = 16
NAT_HD = D_MODEL // NAT_HEADS
NAT_WIN_ROWS = 8
NAT_WIN_COLS = 16
ROPE_THETA = 10000.0
Q_BLOCK = 128
NORM_EPS = 1e-6


def rms_norm(x, g):
    xf = x.astype(jnp.float32)
    y = xf * lax.rsqrt(jnp.mean(xf * xf, axis=-1, keepdims=True) + NORM_EPS)
    return (y * g.astype(jnp.float32)).astype(x.dtype)

def modulate(h, shift, scale):
    return h * (1 + scale) + shift

def swiglu(h, w_in, w_out):
    g, u = jnp.split(h @ w_in, 2, axis=-1)
    return (jax.nn.silu(g) * u) @ w_out

def ffn_step(s, g, shift, scale, gate, w_in, w_out):
    return s + 0.5 * gate * swiglu(modulate(rms_norm(s, g), shift, scale), w_in, w_out)

def pool_mix(h, w, scale):
    b, n, d = h.shape
    hf = h.astype(jnp.float32)
    cs = jnp.concatenate([jnp.zeros((b, 1, d), jnp.float32), jnp.cumsum(hf, axis=1)], axis=1)
    t = jnp.arange(n)
    outs = []
    for gi, win in enumerate(POOL_WINDOWS):
        lo = jnp.clip(t - win // 2, 0, n - 1)
        hi = jnp.clip(t - win // 2 + win - 1, 0, n - 1)
        sl = slice(gi * POOL_GW, (gi + 1) * POOL_GW)
        csg = cs[:, :, sl]
        mean = (csg[:, hi + 1] - csg[:, lo]) / (hi - lo + 1).astype(jnp.float32)[None, :, None]
        outs.append(mean - hf[:, :, sl])
    diff = jnp.stack(outs, axis=2).astype(h.dtype)
    y = jnp.einsum('bngc,gce->bnge', diff, w).reshape(b, n, d)
    return y * scale

def axial_angles(n):
    t = jnp.arange(n)
    rows = (t // GRID_W).astype(jnp.float32)
    cols = (t % GRID_W).astype(jnp.float32)
    per_axis = DIFF_HD // 2
    inv = ROPE_THETA ** (-jnp.arange(0, per_axis, 2, dtype=jnp.float32) / per_axis)
    return rows[:, None] * inv, cols[:, None] * inv

def rotate(x, ang):
    m = x.shape[-1] // 2
    x1, x2 = x[..., :m], x[..., m:]
    cos, sin = jnp.cos(ang), jnp.sin(ang)
    return jnp.concatenate([x1 * cos - x2 * sin, x2 * cos + x1 * sin], axis=-1)

def rope_2d(x, row_ang, col_ang):
    shape = (1, x.shape[1]) + (1,) * (x.ndim - 3) + (row_ang.shape[-1],)
    ra, ca = row_ang.reshape(shape), col_ang.reshape(shape)
    xf = x.astype(jnp.float32)
    half = x.shape[-1] // 2
    out = jnp.concatenate([rotate(xf[..., :half], ra), rotate(xf[..., half:], ca)], axis=-1)
    return out.astype(x.dtype)

def diff_attention(h_lat, h_ctx, w_qkv, lam, subln_g, w_o, lam_init, want_ctx):
    b, n, d = h_lat.shape
    scale = DIFF_HD ** -0.5

    def proj(h):
        q, k, v = jnp.split(h @ w_qkv, 3, axis=-1)
        s = h.shape[:2]
        return (q.reshape(s + (DIFF_HEADS, 2, DIFF_HD)), k.reshape(s + (DIFF_HEADS, 2, DIFF_HD)),
                v.reshape(s + (DIFF_HEADS, 2 * DIFF_HD)))

    q_l, k_l, v_l = proj(h_lat)
    q_c, k_c, v_c = proj(h_ctx)
    ra, ca = axial_angles(n)
    q_l = rope_2d(q_l, ra, ca)
    k_l = rope_2d(k_l, ra, ca)
    lf = lam.astype(jnp.float32)
    lam_full = jnp.exp(jnp.sum(lf[0] * lf[1])) - jnp.exp(jnp.sum(lf[2] * lf[3])) + lam_init

    def attend(q, k, v):
        s = jnp.einsum('bqhjd,bkhjd->bhjqk', q, k).astype(jnp.float32) * scale
        p = jax.nn.softmax(s, axis=-1)
        a = p[:, :, 0] - lam_full * p[:, :, 1]
        return jnp.einsum('bhqk,bkhe->bqhe', a.astype(v.dtype), v)

    k_all = jnp.concatenate([k_l, k_c], axis=1)
    v_all = jnp.concatenate([v_l, v_c], axis=1)
    nb = n // Q_BLOCK
    q_blocks = jnp.moveaxis(q_l.reshape(b, nb, Q_BLOCK, DIFF_HEADS, 2, DIFF_HD), 1, 0)
    o_l = lax.map(lambda qb: attend(qb, k_all, v_all), q_blocks)
    o_l = jnp.moveaxis(o_l, 0, 1).reshape(b, n, DIFF_HEADS, 2 * DIFF_HD)

    def finish(o):
        o = rms_norm(o, subln_g) * (1 - lam_init)
        return o.reshape(o.shape[:2] + (d,)) @ w_o

    out_l = finish(o_l)
    out_c = finish(attend(q_c, k_c, v_c)) if want_ctx else None
    return out_l, out_c

def neighbourhood_attention(h_lat, h_ctx, w_qkv, b_qkv, rpb, w_o, b_o, want_ctx):
    b, n, d = h_lat.shape
    n_rows = n // GRID_W
    wr = min(NAT_WIN_ROWS, n_rows)
    wc = min(NAT_WIN_COLS, GRID_W)
    scale = NAT_HD ** -0.5

    def proj(h):
        q, k, v = jnp.split(h @ w_qkv + b_qkv, 3, axis=-1)
        s = h.shape[:2] + (NAT_HEADS, NAT_HD)
        return q.reshape(s) * scale, k.reshape(s), v.reshape(s)

    q_l, k_l, v_l = proj(h_lat)
    q_c, k_c, v_c = proj(h_ctx)
    gshape = (b, n_rows, GRID_W, NAT_HEADS, NAT_HD)
    k_g = k_l.reshape(gshape)
    v_g = v_l.reshape(gshape)
    q_rows = jnp.moveaxis(q_l.reshape(gshape), 1, 0)
    qcol = jnp.arange(GRID_W)
    col_start = jnp.clip(qcol - wc // 2, 0, GRID_W - wc)
    col_idx = col_start[:, None] + jnp.arange(wc)[None, :]
    col_off = col_idx - qcol[:, None] + (NAT_WIN_COLS - 1)

    def row_block(args):
        r, q = args
        rs = jnp.clip(r - wr // 2, 0, n_rows - wr)
        k_band = lax.dynamic_slice_in_dim(k_g, rs, wr, axis=1)
        v_band = lax.dynamic_slice_in_dim(v_g, rs, wr, axis=1)
        k_win = k_band[:, :, col_idx]
        v_win = v_band[:, :, col_idx]
        row_off = rs + jnp.arange(wr) - r + (NAT_WIN_ROWS - 1)
        bias = rpb[:, row_off[:, None, None], col_off[None, :, :]]
        bias = jnp.transpose(bias, (0, 2, 1, 3)).astype(jnp.float32)
        s_win = jnp.einsum('bqhd,bwqchd->bhqwc', q, k_win).astype(jnp.float32) + bias[None]
        s_ctx = jnp.einsum('bqhd,bkhd->bhqk', q, k_c).astype(jnp.float32)
        s = jnp.concatenate([s_win.reshape(b, NAT_HEADS, GRID_W, wr * wc), s_ctx], axis=-1)
        p = jax.nn.softmax(s, axis=-1).astype(v_win.dtype)
        p_win = p[..., :wr * wc].reshape(b, NAT_HEADS, GRID_W, wr, wc)
        p_ctx = p[..., wr * wc:]
        return (jnp.einsum('bhqwc,bwqchd->bqhd', p_win, v_win)
                + jnp.einsum('bhqk,bkhd->bqhd', p_ctx, v_c))

    o = lax.map(row_block, (jnp.arange(n_rows), q_rows))
    out_l = jnp.moveaxis(o, 0, 1).reshape(b, n, d) @ w_o + b_o
    out_c = None
    if want_ctx:
        s = jnp.einsum('bqhd,bkhd->bhqk', q_c, k_c).astype(jnp.float32)
        p = jax.nn.softmax(s, axis=-1).astype(v_c.dtype)
        o_c = jnp.einsum('bhqk,bkhd->bqhd', p, v_c)
        out_c = o_c.reshape(o_c.shape[0], o_c.shape[1], d) @ w_o + b_o
    return out_l, out_c

def first_inputs(seed: int = 0) -> dict:
    key = jax.random.key(seed)
    ks = jax.random.split(key, 24)
    D = D_MODEL

    def nrm(k, shape, std):
        return jax.random.normal(k, shape, jnp.float32) * std

    return {
        'x': nrm(ks[0], (BATCH, SEQ, D), 1.0),
        'c': nrm(ks[1], (BATCH, D), 1.0),
        'ctx': nrm(ks[2], (BATCH, CTX_LEN, D), 1.0),
        'c_ctx': nrm(ks[3], (D,), 1.0),
        'ada_w': nrm(ks[4], (DEPTH, D, N_MOD * D), 0.5 * D ** -0.5),
        'ada_b': nrm(ks[5], (DEPTH, N_MOD * D), 0.01),
        'norm_g': 1.0 + nrm(ks[6], (DEPTH, 3, D), 0.1),
        'ffn_w_in': nrm(ks[7], (DEPTH, 2, D, 2 * D_FF), D ** -0.5),
        'ffn_w_out': nrm(ks[8], (DEPTH, 2, D_FF, D), D_FF ** -0.5),
        'pool_w': nrm(ks[9], (N_POOL_LAYERS, POOL_GROUPS, POOL_GW, POOL_GW), POOL_GW ** -0.5),
        'pool_scale': 1.0 + nrm(ks[10], (N_POOL_LAYERS, D), 0.1),
        'diff_w_qkv': nrm(ks[11], (N_DIFF_LAYERS, D, 3 * D), D ** -0.5),
        'diff_lam': nrm(ks[12], (N_DIFF_LAYERS, 4, DIFF_HD), 0.1),
        'diff_subln_g': 1.0 + nrm(ks[13], (N_DIFF_LAYERS, 2 * DIFF_HD), 0.1),
        'diff_w_o': nrm(ks[14], (N_DIFF_LAYERS, D, D), D ** -0.5),
        'nat_w_qkv': nrm(ks[15], (N_NAT_LAYERS, D, 3 * D), D ** -0.5),
        'nat_b_qkv': nrm(ks[16], (N_NAT_LAYERS, 3 * D), 0.01),
        'nat_rpb': nrm(ks[17], (N_NAT_LAYERS, NAT_HEADS, 2 * NAT_WIN_ROWS - 1, 2 * NAT_WIN_COLS - 1), 0.1),
        'nat_w_o': nrm(ks[18], (N_NAT_LAYERS, D, D), D ** -0.5),
        'nat_b_o': nrm(ks[19], (N_NAT_LAYERS, D), 0.01),
        'final_g': 1.0 + nrm(ks[20], (D,), 0.1),
    }

def first_block(x, c, ctx, c_ctx, ada_w, ada_b, norm_g, ffn_w_in, ffn_w_out, pool_w, pool_scale,
              diff_w_qkv, diff_lam, diff_subln_g, diff_w_o, nat_w_qkv, nat_b_qkv, nat_rpb,
              nat_w_o, nat_b_o, final_g):
    xc = ctx
    s_c = jax.nn.silu(c)
    s_cc = jax.nn.silu(c_ctx)
    for i in range(DEPTH):
        kind = i % N_MIXERS
        j = i // N_MIXERS
        last = i == DEPTH - 1
        update_ctx = not last
        ctx_needed = update_ctx or kind != 0
        mx = jnp.split((s_c @ ada_w[i] + ada_b[i])[:, None, :], N_MOD, axis=-1)
        mc = jnp.split((s_cc @ ada_w[i] + ada_b[i])[None, None, :], N_MOD, axis=-1)
        x = ffn_step(x, norm_g[i, 0], mx[0], mx[1], mx[2], ffn_w_in[i, 0], ffn_w_out[i, 0])
        if ctx_needed:
            xc = ffn_step(xc, norm_g[i, 0], mc[0], mc[1], mc[2], ffn_w_in[i, 0], ffn_w_out[i, 0])
        hx = modulate(rms_norm(x, norm_g[i, 1]), mx[3], mx[4])
        hc = modulate(rms_norm(xc, norm_g[i, 1]), mc[3], mc[4]) if ctx_needed else None
        if kind == 0:
            ox = pool_mix(hx, pool_w[j], pool_scale[j])
            oc = pool_mix(hc, pool_w[j], pool_scale[j]) if update_ctx else None
        elif kind == 1:
            lam_init = 0.8 - 0.6 * math.exp(-0.3 * i)
            ox, oc = diff_attention(hx, hc, diff_w_qkv[j], diff_lam[j], diff_subln_g[j], diff_w_o[j],
                                    lam_init, update_ctx)
        else:
            ox, oc = neighbourhood_attention(hx, hc, nat_w_qkv[j], nat_b_qkv[j], nat_rpb[j],
                                             nat_w_o[j], nat_b_o[j], update_ctx)
        x = x + mx[5] * ox
        if update_ctx:
            xc = xc + mc[5] * oc
        x = ffn_step(x, norm_g[i, 2], mx[6], mx[7], mx[8], ffn_w_in[i, 1], ffn_w_out[i, 1])
        if update_ctx:
            xc = ffn_step(xc, norm_g[i, 2], mc[6], mc[7], mc[8], ffn_w_in[i, 1], ffn_w_out[i, 1])
    return rms_norm(x, final_g)


N_A_LAYERS = DEPTH // 2
N_B_LAYERS = DEPTH - N_A_LAYERS

LRU_WIDTH = D_MODEL
LRU_BLOCKS = 8
LRU_BLOCK_W = LRU_WIDTH // LRU_BLOCKS
CONV_WIDTH = 4
LRU_C = 8.0

HEAD_DIM = 128
Q_HEADS = D_MODEL // HEAD_DIM
KV_HEADS = 2
Q_PER_KV = Q_HEADS // KV_HEADS
DILATION_GROUPS = ((128, 1), (512, 4), (2048, 16))
N_GROUPS = len(DILATION_GROUPS)
ATT_BLOCK = 128
ROPE_DIM = HEAD_DIM // 4
ROPE_THETA_2 = 500000.0

FFN_HIDDEN = -(-8 * D_MODEL // (3 * 256)) * 256
EPS = 1e-6
NEG_INF = -1e30


def rms_norm_2(x, g):
    x32 = x.astype(jnp.float32)
    y = x32 * lax.rsqrt(jnp.mean(x32 * x32, axis=-1, keepdims=True) + EPS)
    return (y * g.astype(jnp.float32)).astype(x.dtype)

def rope_tables(positions):
    inv_freq = ROPE_THETA_2 ** (-jnp.arange(0, ROPE_DIM, 2, dtype=jnp.float32) / ROPE_DIM)
    ang = positions.astype(jnp.float32)[..., None] * inv_freq
    return jnp.cos(ang), jnp.sin(ang)

def apply_partial_rope(x, cos, sin):
    extra = x.ndim - 3
    shp = cos.shape[:2] + (1,) * extra + cos.shape[-1:]
    c, s = cos.reshape(shp), sin.reshape(shp)
    half = ROPE_DIM // 2
    xr = x[..., :ROPE_DIM].astype(jnp.float32)
    x1, x2 = xr[..., :half], xr[..., half:]
    rot = jnp.concatenate([x1 * c - x2 * s, x2 * c + x1 * s], axis=-1)
    return jnp.concatenate([rot.astype(x.dtype), x[..., ROPE_DIM:]], axis=-1)

def causal_depthwise_conv(x, w, b):
    y = lax.conv_general_dilated(
        x, w[:, None, :].astype(x.dtype), window_strides=(1,),
        padding=((CONV_WIDTH - 1, 0),), dimension_numbers=('NWC', 'WIO', 'NWC'),
        feature_group_count=x.shape[-1])
    return y + b.astype(x.dtype)

def rg_lru(x, w_a, b_a, w_x, b_x, lam):
    B, S, C = x.shape
    x32 = x.astype(jnp.float32)
    xb = x32.reshape(B, S, LRU_BLOCKS, LRU_BLOCK_W)
    r_gate = jax.nn.sigmoid(jnp.einsum('bshi,hij->bshj', xb, w_a.astype(jnp.float32)).reshape(B, S, C) + b_a.astype(jnp.float32))
    i_gate = jax.nn.sigmoid(jnp.einsum('bshi,hij->bshj', xb, w_x.astype(jnp.float32)).reshape(B, S, C) + b_x.astype(jnp.float32))
    log_a = -LRU_C * r_gate * jax.nn.softplus(-lam.astype(jnp.float32))
    a = jnp.exp(log_a)
    u = jnp.sqrt(-jnp.expm1(2.0 * log_a)) * (i_gate * x32)

    def combine(left, right):
        a1, b1 = left
        a2, b2 = right
        return a1 * a2, a2 * b1 + b2

    _, h = lax.associative_scan(combine, (a, u), axis=1)
    return h.astype(x.dtype)

def recurrent_mixer(h, w_in, conv_w, conv_b, ga_w, ga_b, gx_w, gx_b, lam, w_out):
    proj = h @ w_in
    y_branch, x_branch = jnp.split(proj, 2, axis=-1)
    gate = jax.nn.gelu(y_branch, approximate=True)
    xc = causal_depthwise_conv(x_branch, conv_w, conv_b)
    hr = rg_lru(xc, ga_w, ga_b, gx_w, gx_b, lam)
    return (gate * hr) @ w_out

def swiglu_2(h, w_in, w_out):
    g, u = jnp.split(h @ w_in, 2, axis=-1)
    return (jax.nn.silu(g) * u) @ w_out

def shared_kv(h, kv_norm, w_kv, k_norm, cos, sin):
    B, S, _ = h.shape
    hn = rms_norm_2(h, kv_norm)
    kv = (hn @ w_kv).reshape(B, S, N_GROUPS, 2, KV_HEADS, HEAD_DIM)
    k, v = kv[:, :, :, 0], kv[:, :, :, 1]
    k = rms_norm_2(k, k_norm[:, None, :])
    k = apply_partial_rope(k, cos, sin)
    return k, v

def dilated_window_attention(q, k, v, window, dilation):
    B, S = q.shape[:2]
    n_keys = window // dilation
    span = dilation * ATT_BLOCK
    S_pad = -(-S // span) * span
    L = S_pad // dilation
    nb = L // ATT_BLOCK
    pad = S_pad - S

    def to_phase(t):
        t = jnp.pad(t, [(0, 0), (0, pad)] + [(0, 0)] * (t.ndim - 2))
        t = t.reshape((B, L, dilation) + t.shape[2:])
        t = jnp.moveaxis(t, 2, 1)
        return t.reshape((B, dilation, nb, ATT_BLOCK) + t.shape[3:])

    def with_prev(t):
        prev = jnp.pad(t, [(0, 0), (0, 0), (1, 0)] + [(0, 0)] * (t.ndim - 3))[:, :, :-1]
        return jnp.concatenate([prev, t], axis=3)

    qp = to_phase(q)
    kb = with_prev(to_phase(k))
    vb = with_prev(to_phase(v))
    s = jnp.einsum('bpnqhgd,bpnkhd->bpnhgqk', qp, kb).astype(jnp.float32) * (HEAD_DIM ** -0.5)
    q_idx = jnp.arange(ATT_BLOCK)[:, None] + ATT_BLOCK
    k_idx = jnp.arange(2 * ATT_BLOCK)[None, :]
    dist = q_idx - k_idx
    band = (dist >= 0) & (dist <= n_keys)
    has_prev = (jnp.arange(nb)[:, None, None] > 0) | (k_idx >= ATT_BLOCK)[None]
    mask = band[None] & has_prev
    s = jnp.where(mask[None, None, :, None, None], s, NEG_INF)
    m = jnp.max(s, axis=-1, keepdims=True)
    p = jnp.exp(s - m)
    den = jnp.sum(p, axis=-1, keepdims=True)
    o = jnp.einsum('bpnhgqk,bpnkhd->bpnqhgd', (p / den).astype(v.dtype), vb)
    lse = jnp.moveaxis((m + jnp.log(den))[..., 0], -1, 3)

    def from_phase(t):
        t = t.reshape((B, dilation, L) + t.shape[4:])
        t = jnp.moveaxis(t, 1, 2).reshape((B, S_pad) + t.shape[3:])
        return t[:, :S]

    return from_phase(o), from_phase(lse)

def dilated_attention_mixer(h, w_q, q_norm, w_o, k, v, cos, sin):
    B, S, _ = h.shape
    q = (h @ w_q).reshape(B, S, N_GROUPS, Q_HEADS, HEAD_DIM)
    q = rms_norm_2(q, q_norm[:, None, :])
    q = apply_partial_rope(q, cos, sin)
    q = q.reshape(B, S, N_GROUPS, KV_HEADS, Q_PER_KV, HEAD_DIM)
    outs, lses = [], []
    for g, (window, dilation) in enumerate(DILATION_GROUPS):
        o, l = dilated_window_attention(q[:, :, g], k[:, :, g], v[:, :, g], window, dilation)
        outs.append(o)
        lses.append(l)
    wts = jax.nn.softmax(jnp.stack(lses, axis=0), axis=0)
    o = jnp.sum(wts[..., None] * jnp.stack(outs, axis=0).astype(jnp.float32), axis=0).astype(h.dtype)
    return o.reshape(B, S, Q_HEADS * HEAD_DIM) @ w_o

def second_inputs(seed: int = 0) -> dict:
    key = jax.random.key(seed)
    ks = jax.random.split(key, 32)

    def nrm(k, shape, fan_in):
        return jax.random.normal(k, shape, jnp.float32) * (fan_in ** -0.5)

    def gain(k, shape):
        return 1.0 + 0.05 * jax.random.normal(k, shape, jnp.float32)

    def bias(k, shape):
        return 0.01 * jax.random.normal(k, shape, jnp.float32)

    nA, nB = N_A_LAYERS, N_B_LAYERS
    a8 = jax.random.uniform(ks[9], (nA, LRU_WIDTH), jnp.float32, 0.9, 0.999)
    a0 = a8 ** (1.0 / LRU_C)
    lam = jnp.log(a0) - jnp.log1p(-a0)
    return {
        "x": jax.random.normal(ks[0], (BATCH, SEQ, D_MODEL), jnp.float32),
        "positions": jnp.broadcast_to(jnp.arange(SEQ, dtype=jnp.int32)[None, :], (BATCH, SEQ)),
        "a_norm": gain(ks[1], (nA, D_MODEL)),
        "a_w_in": nrm(ks[2], (nA, D_MODEL, 2 * LRU_WIDTH), D_MODEL),
        "a_conv_w": nrm(ks[3], (nA, CONV_WIDTH, LRU_WIDTH), CONV_WIDTH),
        "a_conv_b": bias(ks[4], (nA, LRU_WIDTH)),
        "a_gate_a_w": nrm(ks[5], (nA, LRU_BLOCKS, LRU_BLOCK_W, LRU_BLOCK_W), LRU_BLOCK_W),
        "a_gate_a_b": bias(ks[6], (nA, LRU_WIDTH)),
        "a_gate_x_w": nrm(ks[7], (nA, LRU_BLOCKS, LRU_BLOCK_W, LRU_BLOCK_W), LRU_BLOCK_W),
        "a_gate_x_b": bias(ks[8], (nA, LRU_WIDTH)),
        "a_lambda": lam,
        "a_w_out": nrm(ks[10], (nA, LRU_WIDTH, D_MODEL), LRU_WIDTH),
        "a_ffn_norm": gain(ks[11], (nA, D_MODEL)),
        "a_ffn_w_in": nrm(ks[12], (nA, D_MODEL, 2 * FFN_HIDDEN), D_MODEL),
        "a_ffn_w_out": nrm(ks[13], (nA, FFN_HIDDEN, D_MODEL), FFN_HIDDEN),
        "kv_norm": gain(ks[14], (D_MODEL,)),
        "w_kv": nrm(ks[15], (D_MODEL, N_GROUPS * 2 * KV_HEADS * HEAD_DIM), D_MODEL),
        "k_norm": gain(ks[16], (N_GROUPS, HEAD_DIM)),
        "b_norm": gain(ks[17], (nB, D_MODEL)),
        "b_w_q": nrm(ks[18], (nB, D_MODEL, N_GROUPS * Q_HEADS * HEAD_DIM), D_MODEL),
        "b_q_norm": gain(ks[19], (nB, N_GROUPS, HEAD_DIM)),
        "b_w_o": nrm(ks[20], (nB, Q_HEADS * HEAD_DIM, D_MODEL), Q_HEADS * HEAD_DIM),
        "b_ffn_norm": gain(ks[21], (nB, D_MODEL)),
        "b_ffn_w_in": nrm(ks[22], (nB, D_MODEL, 2 * FFN_HIDDEN), D_MODEL),
        "b_ffn_w_out": nrm(ks[23], (nB, FFN_HIDDEN, D_MODEL), FFN_HIDDEN),
    }

def second_block(x, positions, a_norm, a_w_in, a_conv_w, a_conv_b, a_gate_a_w, a_gate_a_b,
              a_gate_x_w, a_gate_x_b, a_lambda, a_w_out, a_ffn_norm, a_ffn_w_in, a_ffn_w_out,
              kv_norm, w_kv, k_norm, b_norm, b_w_q, b_q_norm, b_w_o, b_ffn_norm, b_ffn_w_in,
              b_ffn_w_out):
    cos, sin = rope_tables(positions)
    h = x
    k = v = None
    for layer in range(DEPTH):
        if layer < N_A_LAYERS:
            i = layer
            h = h + recurrent_mixer(rms_norm_2(h, a_norm[i]), a_w_in[i], a_conv_w[i], a_conv_b[i],
                                    a_gate_a_w[i], a_gate_a_b[i], a_gate_x_w[i], a_gate_x_b[i],
                                    a_lambda[i], a_w_out[i])
            h = h + swiglu_2(rms_norm_2(h, a_ffn_norm[i]), a_ffn_w_in[i], a_ffn_w_out[i])
        else:
            if layer == N_A_LAYERS:
                k, v = shared_kv(h, kv_norm, w_kv, k_norm, cos, sin)
            j = layer - N_A_LAYERS
            h = h + dilated_attention_mixer(rms_norm_2(h, b_norm[j]), b_w_q[j], b_q_norm[j], b_w_o[j],
                                            k, v, cos, sin)
            h = h + swiglu_2(rms_norm_2(h, b_ffn_norm[j]), b_ffn_w_in[j], b_ffn_w_out[j])
    return h


def setup_inputs(seed=0):
    out = dict(first_inputs(seed))
    for name, value in second_inputs(seed + 1).items():
        if name != "x":
            out[name + "_2"] = value
    return out


def reference(
    x, c, ctx, c_ctx, ada_w, ada_b, norm_g, ffn_w_in, ffn_w_out, pool_w, pool_scale, diff_w_qkv,
    diff_lam, diff_subln_g, diff_w_o, nat_w_qkv, nat_b_qkv, nat_rpb, nat_w_o, nat_b_o, final_g,
    positions_2, a_norm_2, a_w_in_2, a_conv_w_2, a_conv_b_2, a_gate_a_w_2, a_gate_a_b_2,
    a_gate_x_w_2, a_gate_x_b_2, a_lambda_2, a_w_out_2, a_ffn_norm_2, a_ffn_w_in_2,
    a_ffn_w_out_2, kv_norm_2, w_kv_2, k_norm_2, b_norm_2, b_w_q_2, b_q_norm_2, b_w_o_2,
    b_ffn_norm_2, b_ffn_w_in_2, b_ffn_w_out_2,
):
    x = first_block(
        x, c, ctx, c_ctx, ada_w, ada_b, norm_g, ffn_w_in, ffn_w_out, pool_w, pool_scale,
        diff_w_qkv, diff_lam, diff_subln_g, diff_w_o, nat_w_qkv, nat_b_qkv, nat_rpb, nat_w_o,
        nat_b_o, final_g,
    )
    return second_block(
        x, positions_2, a_norm_2, a_w_in_2, a_conv_w_2, a_conv_b_2, a_gate_a_w_2, a_gate_a_b_2,
        a_gate_x_w_2, a_gate_x_b_2, a_lambda_2, a_w_out_2, a_ffn_norm_2, a_ffn_w_in_2,
        a_ffn_w_out_2, kv_norm_2, w_kv_2, k_norm_2, b_norm_2, b_w_q_2, b_q_norm_2, b_w_o_2,
        b_ffn_norm_2, b_ffn_w_in_2, b_ffn_w_out_2,
    )


_drawn_inputs = setup_inputs


def setup_inputs(seed=0):
    import zlib

    import numpy as np

    out = dict(_drawn_inputs(seed))
    spreads = {}
    factors = {'a_gate_a_b_2': 8.0,
     'a_gate_x_b_2': 8.0,
     'kv_norm_2': 4.809,
     'k_norm_2': 7.39,
     'b_norm_2': 8.0,
     'b_q_norm_2': 8.0,
     'b_ffn_norm_2': 6.532}
    for name, (base, spread) in spreads.items():
        noise = np.random.default_rng([zlib.crc32(name.encode()), seed]).standard_normal(out[name].shape)
        drawn = base * np.exp(spread * noise) if base else spread * noise
        out[name] = __import__('jax').numpy.asarray(drawn.astype(out[name].dtype))
    for name, factor in factors.items():
        out[name] = (out[name] * factor).astype(out[name].dtype)
    return out
```

```python
import math
from contextlib import ExitStack

import numpy as np

import concourse.bass as bass
from concourse import mybir

ALU = mybir.AluOpType
ACT = mybir.ActivationFunctionType
AX = mybir.AxisListType
F32 = mybir.dt.float32
F32R = mybir.dt.float32r
I32 = mybir.dt.int32

P = 128
D = 1024
DC = D // P
T = 256
TT = T // P
F = 2816
FC = F // P
W_OUT_PARTS = (8, 7, 7)
EPS = 1e-6
RING = 4
AHEAD = RING - 1
HEADS = 8
LAM_INIT = 0.8 - 0.6 * math.exp(-0.3)
DIFF_SCALE = 64 ** -0.5
DIL_SCALE = 128 ** -0.5
NEG = -1e30
N_MODS = 18
MODS_FIRST = 2

STAGES = [
    dict(kind="ffn", norm=0, mod=0, n=2 * T, ada=(2, 13)),
    dict(kind="pool", norm=1, mod=3, n=2 * T),
    dict(kind="ffn", norm=2, mod=6, n=2 * T, ada=(13, 18)),
    dict(kind="ffn", norm=3, mod=9, n=2 * T, ada=None),
    dict(kind="diff", norm=4, mod=12, n=2 * T),
    dict(kind="ffn", norm=5, mod=15, n=T, ada=None),
    dict(kind="final", n=T),
    dict(kind="lru", n=T),
    dict(kind="ffn", gain="a_ffn", mod=None, n=T, ada=None),
    dict(kind="dil", n=T),
    dict(kind="ffn", gain="b_ffn", mod=None, n=T, ada=None),
]
UNITS = dict(ffn=2 * FC + DC * 3, pool=2, diff=24 + 8, final=0, lru=16 + 2 + 8, dil=12 + 24 + 8)
CHUNKS = dict(ffn=2 * FC + DC, pool=DC, diff=DC, final=0, lru=16 + DC, dil=DC)
GROUPS = dict(diff=6, dil=9)
T_SETS = dict(ffn=1, pool=2, diff=1, lru=1, dil=2)
H_SETS = dict(ffn=1, pool=1, diff=1, lru=1, dil=2)


def plan():
    u = c = norms = ts = hs = p = f = 0
    for s in STAGES:
        s.update(u0=u, c0=c, norm_i=norms, t0=ts * DC, h0=hs * DC, p0=p, f0=f)
        u += UNITS[s["kind"]]
        c += CHUNKS[s["kind"]]
        norms += 1
        ts += T_SETS.get(s["kind"], 0)
        hs += H_SETS.get(s["kind"], 0)
        p += GROUPS.get(s["kind"], 0)
        f += FC if s["kind"] == "ffn" else 0
    return u


VEC = {}


def vec_columns():
    at = 0
    for name, n in (("c", 16), ("ada_b", 144), ("norm_g", 48), ("pool_scale", 8), ("final_g", 8),
                    ("a_norm", 8), ("conv_w", 32), ("conv_b", 8), ("ga_b", 8), ("gx_b", 8), ("lam", 8),
                    ("a_ffn", 8), ("kv_norm", 8), ("b_norm", 8), ("b_ffn", 8), ("diff_lam", 256)):
        VEC[name] = (at, n)
        at += n
    return at


NV = vec_columns()


class Tally:

    def __init__(self, eng, sem):
        self.eng, self.sem, self.n, self.marks = eng, sem, 0, 0

    def mark(self, ins):
        ins.then_inc(self.sem, 1)
        self.n = self.n + 1
        self.marks += 1

    def sync(self):
        self.eng.wait_ge(self.sem, self.n)

    def loop(self, first, end, per, body):
        base = self.n
        if end - first == 1:
            body(first)
        else:
            with self.eng.Fori(first, end) as i:
                self.n = base + (i - first) * per
                before = self.marks
                body(i)
                assert self.marks - before == per, (self.marks - before, per)
        self.n = base + (end - first) * per


def loop(eng, first, end, body):
    if end - first == 1:
        body(first)
    elif end > first:
        with eng.Fori(first, end) as i:
            body(i)


def build(nc, a, out, stages=None):
    TOTAL = plan()
    stages = STAGES if stages is None else STAGES[:stages]
    TOTAL = stages[-1]["u0"] + UNITS[stages[-1]["kind"]]

    with ExitStack() as ctx:
        def sb(name, shape, dt=F32, c=ctx):
            return c.enter_context(nc.sbuf_tensor(name, shape, dt))

        def sem(name):
            return ctx.enter_context(nc.semaphore(name))

        X = sb("X", [P, DC, 2 * T])
        H_hi = sb("H_hi", [P, DC, 2 * T], F32R)
        H_lo = sb("H_lo", [P, DC, 2 * T], F32R)
        raw = sb("raw", [P, RING, D])
        W_hi = sb("W_hi", [P, RING, D], F32R)
        W_lo = sb("W_lo", [P, RING, D], F32R)
        ada_w = sb("ada_w", [P, 2, D])
        vec = sb("vec", [P, NV])
        ident = sb("ident", [P, P])
        ones = sb("ones", [P, P])
        silu_c = sb("silu_c", [P, DC, 32])
        mods = sb("mods", [P, N_MODS, DC, 2])
        ada_T = sb("ada_T", [P, DC, 32])
        gain = sb("gain", [P, DC, 2])
        gate = sb("gate", [P, DC, 2])
        ssq = sb("ssq", [P, 2 * T])
        work = sb("work", [P, 3, 2 * T])
        std = sb("std", [P, 4])
        rstd = sb("rstd", [P, 4])
        sp8 = sb("sp8", [P, DC])
        nsp8 = sb("nsp8", [P, DC])
        lam = sb("lam", [P, 4])
        b_cos = sb("b_cos", [P, TT, 32])
        b_sin = sb("b_sin", [P, TT, 32])
        stat = sb("stat", [P, 64])
        with ExitStack() as c:
            G_hi = sb("G_hi", [P, FC, 2 * T], F32R, c)
            G_lo = sb("G_lo", [P, FC, 2 * T], F32R, c)
        with ExitStack() as c:
            sp_t = sb("sp_t", [P, 4, DC], F32, c)
            pos = sb("pos", [P, TT], I32, c)
            posf = sb("posf", [P, TT], F32, c)
            inv_freq = sb("inv_freq", [P, 16], F32, c)
            trig = sb("trig", [P, 5, TT, 16], F32, c)
            dots = sb("dots", [P, 2, 64], F32, c)
            ada_first = sb("ada_first", [P, MODS_FIRST * 8, D], F32, c)
        PAD = 8
        with ExitStack() as c:
            pool_h = sb("pool_h", [P, DC, 2, T + 2 * PAD], F32, c)
            pool_s = sb("pool_s", [P, 2, 2, 2, T + 2 * PAD], F32, c)
            pool_n = sb("pool_n", [P, 4, T], F32, c)
        with ExitStack() as c:
            d_KN = sb("d_KN", [P, 4, D], F32, c)
            d_QN = sb("d_QN", [P, TT, D], F32, c)
            d_VN = sb("d_VN", [P, 4, D], F32, c)
            d_KT = sb("d_KT", [P, HEADS, 2 * T], F32, c)
            d_QT = sb("d_QT", [P, HEADS, T], F32, c)
            d_P = sb("d_P", [P, 2, 2, 2 * T], F32, c)
            d_A = sb("d_A", [P, 2, 2 * T], F32, c)
            d_AT = sb("d_AT", [P, 2, 4, P], F32, c)
            d_cos = sb("d_cos", [P, TT, 64], F32, c)
            d_sin = sb("d_sin", [P, TT, 64], F32, c)
            d_g = sb("d_g", [P, P], F32, c)
        d_ON = d_KN[:, 0:TT, :]
        with ExitStack() as c:
            l_G = sb("l_G", [P, DC, T], F32, c)
            l_XB = sb("l_XB", [P, DC, T + 3], F32, c)
            l_XC = sb("l_XC", [P, DC, T], F32, c)
            l_R = sb("l_R", [P, DC, T], F32, c)
            l_I = sb("l_I", [P, DC, T], F32, c)
            l_A = sb("l_A", [P, DC, T], F32, c)
            l_T = sb("l_T", [P, DC, T], F32, c)
            l_H = sb("l_H", [P, DC, T], F32, c)
        with ExitStack() as c:
            b_N = sb("b_N", [P, 2, TT, 512], F32, c)
            b_VN = sb("b_VN", [P, TT, 3, T], F32, c)
            b_KT = sb("b_KT", [P, 6, T], F32, c)
            b_QT = sb("b_QT", [P, 24, T], F32, c)
            b_S = sb("b_S", [P, 2, 768], F32, c)
            b_PT = sb("b_PT", [P, 2, 768], F32, c)
            b_mask = sb("b_mask", [P, TT, 768], F32, c)
            b_gk = sb("b_gk", [P, 3, P], F32, c)
            b_gq = sb("b_gq", [P, 3, P], F32, c)
            b_ra = sb("b_ra", [P, TT, 4, 32], F32, c)
            b_rb = sb("b_rb", [P, TT, 4, 32], F32, c)

        PS = ctx.enter_context(nc.psum_tensor("PS", [P, 8, 512], F32))
        PSf = PS[:, :, :].rearrange("p b n -> p (b n)")
        ADA_BANK, SUM_BANK, BC_BANK = 4, 6, 7

        raw_ld = [sem(f"raw_ld{i}") for i in range(RING)]
        hi_ready = sem("hi_ready")
        lo_ready = sem("lo_ready")
        unit_done = sem("unit_done")
        psum_free = sem("psum_free")
        proj_taken = sem("proj_taken")
        ada_ld = [sem(f"ada_ld{i}") for i in range(2)]
        ada_used = sem("ada_used")
        first_ld = [sem(f"first_ld{i}") for i in range(4)]
        first_used = sem("first_used")
        ada_taken = sem("ada_taken")
        in_vec, in_x, in_c = sem("in_vec"), sem("in_x"), sem("in_c")
        silu_c_ready = sem("silu_c_ready")
        start_ready = sem("start_ready")
        ssq_ready = sem("ssq_ready")
        norm_pe, norm_sd, norm_rs = sem("norm_pe"), sem("norm_sd"), sem("norm_rs")
        t_ready = sem("t_ready")
        h_hi_ready = sem("h_hi_ready")
        h_ready = sem("h_ready")
        silu_ready = sem("silu_ready")
        gu_ready = sem("gu_ready")
        vself = sem("vself")
        start_act = sem("start_act")
        in_pos = sem("in_pos")
        stage_ld = sem("stage_ld")
        region_free = sem("region_free")
        kn_ready = sem("kn_ready")
        tp_done = sem("tp_done")
        tp_taken = sem("tp_taken")
        s_done, nb_ready, p_ready, a_ready = sem("s_done"), sem("nb_ready"), sem("p_ready"), sem("a_ready")
        o_done, o_hi, o_taken = sem("o_done"), sem("o_hi"), sem("o_taken")
        o_sd, on_ready, ot_done = sem("o_sd"), sem("on_ready"), sem("ot_done")
        oh_hi, oh_ready = sem("oh_hi"), sem("oh_ready")
        gelu_done, xc_ready, xc_hi, xc_lo = sem("gelu_done"), sem("xc_ready"), sem("xc_hi"), sem("xc_lo")
        sig_done, a_t_done, om_ready, sqrt_done = sem("sig_done"), sem("a_t_done"), sem("om_ready"), sem("sqrt_done")
        y_ready, y_hi, y_lo = sem("y_ready"), sem("y_hi"), sem("y_lo")
        sq_done, ss_ready, sd_done = sem("sq_done"), sem("ss_ready"), sem("sd_done")
        stored = sem("stored")

        def V(name):
            at, n = VEC[name]
            return vec[:, at:at + n]

        def gain_of(s, d, h):
            if s.get("mod") is None:
                return V(s["gain"])[:, d:d + 1]
            return gain[:, d, h:h + 1]

        def halves(n):
            return [(0, slice(0, T))] + ([(1, slice(T, 2 * T))] if n > T else [])

        block = ctx.enter_context(nc.Block())

        @block.sync
        def _(sp):
            sp.dma_start(vec[:, :], a["vec"]).then_inc(in_vec, 16)
            sp.dma_start(ident[:, :], a["ident"]).then_inc(in_c, 16)
            sp.dma_start(pos[:, :], a["positions"]).then_inc(in_pos, 16)
            sp.dma_start(inv_freq[:, :], a["inv_freq"]).then_inc(in_pos, 16)
            sp.dma_start(X[:, :, :], a["xT"]).then_inc(in_x, 16)
            n4 = MODS_FIRST * 8 // 4
            for q in range(4):
                sp.dma_start(ada_first[:, n4 * q:n4 * q + n4, :],
                             a["ada_w"][n4 * q:n4 * q + n4].rearrange("m p d -> p m d")).then_inc(first_ld[q], 16)

            def load(u, slot, blocks=8):
                sp.wait_ge(lo_ready, u + 1)
                sp.dma_start(raw[:, slot, 0:blocks * P], a["w"][u, :, 0:blocks * P]).then_inc(raw_ld[slot], 16)

            def units(u0, n):
                def body(i):
                    for k in range(4):
                        load(u0 + 4 * i + k, (u0 + k) % RING)
                loop(sp, 0, n // 4, body)
                for k in range(n - n % 4, n):
                    load(u0 + k, (u0 + k) % RING)

            for s in stages:
                if s["kind"] == "ffn":
                    units(s["u0"], 2 * FC)
                    u1 = s["u0"] + 2 * FC

                    def body(i):
                        for k in range(4):
                            for part, blocks in enumerate(W_OUT_PARTS):
                                load(u1 + 12 * i + 3 * k + part, (u1 + 3 * k + part) % RING, blocks)
                    loop(sp, 0, 2, body)
                else:
                    units(s["u0"], UNITS[s["kind"]])
            last = stages[-1]
            for d in range(DC):
                sp.wait_ge(psum_free, RING + last["c0"] + CHUNKS[last["kind"]] - DC + d + 1)
                sp.dma_start(out[:, d, :], X[:, d, 0:out.shape[2]]).then_inc(stored, 16)
            sp.wait_ge(stored, 16 * DC)

        @block.gpsimd
        def _(pool):
            def mod_weights(m):
                for part in range(8):
                    pool.wait_ge(ada_used, (m - MODS_FIRST) * 8 + (part + 1))
                    pool.dma_start(ada_w[:, part % 2, :], a["ada_w"][m * 8 + part]).then_inc(ada_ld[part % 2], 16)

            pool.wait_ge(first_used, 8)
            turn = 0
            for s in stages:
                if s.get("ada"):
                    loop(pool, s["ada"][0], s["ada"][1], mod_weights)
                consts = {
                    "pool": [(pool_n[:, :, :], "pool_n")],
                    "diff": [(d_cos[:, :, :], "d_cos"), (d_sin[:, :, :], "d_sin"), (d_g[:, :], "subln_g")],
                    "dil": [(b_mask[:, :, :], "mask"), (b_gk[:, :, :], "k_norm"), (b_gq[:, :, :], "q_norm")],
                }.get(s["kind"], [])
                if consts:
                    turn += 1
                    pool.wait_ge(region_free, turn)
                    for dst, name in consts:
                        pool.dma_start(dst, a[name]).then_inc(stage_ld, 16)

        @block.tensor
        def _(pe):
            pe.sem_inc(unit_done, RING)
            pe.sem_inc(ada_used, 2)

            def block3(out, slot, b, hi, lo, start, stop):
                w = slice(b * P, (b + 1) * P)
                pe.matmul(out, W_hi[:, slot, w], hi, start=start, stop=False)
                pe.matmul(out, W_hi[:, slot, w], lo, start=False, stop=False)
                return pe.matmul(out, W_lo[:, slot, w], hi, start=False, stop=stop)

            def ada_products(part, weights):
                for j in range(4):
                    mm = pe.matmul(PS[32 * j:32 * j + 32, ADA_BANK, 0:256], silu_c[:, part, :],
                                   weights[:, 256 * j:256 * j + 256], start=part == 0, stop=part == 7)
                return mm

            def ada_part(m, part):
                if part == 0:
                    pe.wait_ge(ada_taken, m)
                pe.wait_ge(ada_ld[part % 2], 16 * ((m - MODS_FIRST) * 4 + (part // 2 + 1)))
                ada_products(part, ada_w[:, part % 2, :]).then_inc(ada_used, 1)

            def norm(s, n):
                k = s["norm_i"]
                pe.wait_ge(ssq_ready, DC * (k + 1))
                for t in range(n // P):
                    mm = pe.matmul(PS[:, SUM_BANK, t:t + 1], ssq[:, t * P:(t + 1) * P], ones[:, 0:1],
                                   start=True, stop=True)
                mm.then_inc(norm_pe, 1)
                pe.wait_ge(norm_rs, k + 1)
                for t in range(n // P):
                    mm = pe.matmul(PS[:, BC_BANK, t * P:(t + 1) * P], rstd[:, t:t + 1].to_broadcast([P, P]),
                                   ident[:, :], start=True, stop=True)
                mm.then_inc(norm_pe, 1)

            def linear(u0, c0, n_units, lo, hi, h_sem, h_base, h_per, ada=None):
                def unit(u, c, k, kc_wait=False):
                    pe.wait_ge(psum_free, c + 1)
                    pe.wait_ge(lo_ready, RING + (u + 1))
                    for kc in range(DC):
                        mm = block3(PS[:, (c0 + k) % RING, 0:hi - lo], (u0 + k) % RING, kc,
                                    H_hi[:, kc, lo:hi], H_lo[:, kc, lo:hi], kc == 0, kc == DC - 1)
                    mm.then_inc(unit_done, 1)

                def mod_parts(m, k):
                    ada_part(m, 2 * k)
                    ada_part(m, 2 * k + 1)

                for k in range(3):
                    pe.wait_ge(psum_free, c0 + k + 1)
                    pe.wait_ge(lo_ready, RING + u0 + k + 1)
                for kc in range(DC):
                    pe.wait_ge(h_sem, h_base + h_per * (kc + 1))
                    for k in range(3):
                        mm = block3(PS[:, (c0 + k) % RING, 0:hi - lo], (u0 + k) % RING, kc,
                                    H_hi[:, kc, lo:hi], H_lo[:, kc, lo:hi], kc == 0, kc == DC - 1)
                        if kc == DC - 1:
                            mm.then_inc(unit_done, 1)
                    if ada:
                        ada_part(ada[0], kc)
                unit(u0 + 3, c0 + 3, 3)

                def body(i, with_ada=False):
                    for k in range(4):
                        unit(u0 + 4 * i + k, c0 + 4 * i + k, k)
                        if with_ada:
                            mod_parts(ada[0] + i, k)
                n_ada = ada[1] - ada[0] if ada else 0
                if n_ada > 1:
                    loop(pe, 1, n_ada, lambda i: body(i, True))
                loop(pe, max(n_ada, 1), n_units // 4, body)

            def w_out(s, n):
                u1, c1 = s["u0"] + 2 * FC, s["c0"] + 2 * FC
                pe.wait_ge(gu_ready, 1 + s["f0"] + W_OUT_PARTS[0] + W_OUT_PARTS[1])

                def body(i):
                    for k in range(4):
                        pe.wait_ge(psum_free, c1 + 4 * i + (k + 1))
                        f = 0
                        for part, blocks in enumerate(W_OUT_PARTS):
                            pe.wait_ge(lo_ready, RING + u1 + 12 * i + (3 * k + part + 1))
                            if part == 2:
                                pe.wait_ge(gu_ready, 1 + s["f0"] + FC)
                            for b in range(blocks):
                                mm = block3(PS[:, (c1 + k) % RING, 0:n], (u1 + 3 * k + part) % RING, b,
                                            G_hi[:, f, 0:n], G_lo[:, f, 0:n], f == 0, f == FC - 1)
                                f += 1
                            mm.then_inc(unit_done, 1)
                loop(pe, 0, 2, body)

            def project(s, g, tiles, first_bank, col, h_wait=None):
                p = s["p0"] + g
                pe.wait_ge(proj_taken, p + 1)
                if h_wait:
                    pe.wait_ge(h_ready, h_wait)
                for q in range(4):
                    u = s["u0"] + 4 * g + q
                    pe.wait_ge(lo_ready, RING + u + 1)
                    for t in range(tiles):
                        for k2 in range(2):
                            kc = 2 * q + k2
                            rows = slice(col + t * P, col + (t + 1) * P)
                            w = slice(k2 * 512, (k2 + 1) * 512)
                            o = PS[:, first_bank + t, :]
                            pe.matmul(o, H_hi[:, kc, rows], W_hi[:, u % RING, w], start=kc == 0, stop=False)
                            pe.matmul(o, H_hi[:, kc, rows], W_lo[:, u % RING, w], start=False, stop=False)
                            mm = pe.matmul(o, H_lo[:, kc, rows], W_hi[:, u % RING, w], start=False, stop=kc == 7)
                    mm.then_inc(unit_done, 1)

            n4 = MODS_FIRST * 8 // 4
            pe.wait_ge(silu_c_ready, 1)
            pe.wait_ge(in_c, 16)
            norm(stages[0], 2 * T)
            for m in range(MODS_FIRST):
                if m:
                    pe.wait_ge(ada_taken, m)
                for part in range(8):
                    if (8 * m + part) % n4 == 0:
                        pe.wait_ge(first_ld[(8 * m + part) // n4], 16)
                    ada_products(part, ada_first[:, 8 * m + part, :]).then_inc(first_used, 1)

            tp = 0
            its = 0
            for s in stages:
                n = s["n"]
                if s["kind"] == "ffn":
                    if s is not stages[0]:
                        norm(s, n)
                    linear(s["u0"], s["c0"], 2 * FC, 0, n, h_ready, s["h0"], 1, s["ada"])
                    w_out(s, n)

                elif s["kind"] == "pool":
                    norm(s, n)
                    for half in range(2):
                        u = s["u0"] + half
                        pe.wait_ge(lo_ready, RING + u + 1)
                        for k in range(4):
                            c = 4 * half + k
                            pe.wait_ge(psum_free, s["c0"] + c + 1)
                            for k2 in range(2):
                                kc = 2 * (c // 2) + k2
                                pe.wait_ge(h_ready, s["h0"] + kc + 1)
                                mm = block3(PS[:, (s["c0"] + c) % RING, 0:n], u % RING, 2 * k + k2,
                                            H_hi[:, kc, 0:n], H_lo[:, kc, 0:n], k2 == 0, k2 == 1)
                        mm.then_inc(unit_done, 1)

                elif s["kind"] == "diff":
                    norm(s, n)
                    for g in range(6):
                        project(s, g, 4 if g < 4 else TT, 4 * (g % 2), 0, s["h0"] + DC if g == 0 else None)
                    for h in range(HEADS):
                        if h == 0:
                            pe.wait_ge(kn_ready, 6)
                            pe.wait_ge(proj_taken, s["p0"] + 6 + 2)
                            pe.wait_ge(in_c, 16)
                        pe.wait_ge(tp_taken, tp + 1)
                        for t in range(4):
                            mm = pe.transpose(PS[:, 4 + tp % 2, t * P:(t + 1) * P],
                                              d_KN[:, t, h * P:(h + 1) * P], ident[:, :])
                        mm.then_inc(tp_done, 1)
                        tp += 1
                    for hh in range(HEADS // 2):
                        pe.wait_ge(tp_taken, tp + 1)
                        for h2 in range(2):
                            for t in range(TT):
                                mm = pe.transpose(PS[:, 4 + tp % 2, (2 * h2 + t) * P:(2 * h2 + t + 1) * P],
                                                  d_QN[:, t, (2 * hh + h2) * P:(2 * hh + h2 + 1) * P], ident[:, :])
                        mm.then_inc(tp_done, 1)
                        tp += 1
                    pe.wait_ge(tp_taken, tp + 2)

                    def scores(it):
                        h, qt = divmod(it, TT)
                        if it >= 2:
                            pe.wait_ge(p_ready, its + it - 1)
                        for j in range(2):
                            rows = slice(64 * j, 64 * j + 64)
                            mm = pe.matmul(PS[:, 2 * (it % 2) + j, :], d_QT[rows, h, qt * P:(qt + 1) * P],
                                           d_KT[rows, h, :], start=True, stop=True)
                        mm.then_inc(s_done, 1)

                    def turn_p(it):
                        nonlocal tp
                        pe.wait_ge(a_ready, its + it + 1)
                        pe.wait_ge(tp_taken, tp + 1)
                        for k in range(4):
                            mm = pe.transpose(PS[:, 4 + tp % 2, k * P:(k + 1) * P],
                                              d_A[:, it % 2, k * P:(k + 1) * P], ident[:, :])
                        mm.then_inc(tp_done, 1)
                        tp += 1

                    def values(it, tp_of):
                        h, qt = divmod(it, TT)
                        pe.wait_ge(tp_taken, tp_of + 3)
                        if it >= 2:
                            pe.wait_ge(o_taken, its + it - 1)
                        for k in range(4):
                            mm = pe.matmul(PS[:, 6 + it % 2, 0:P], d_AT[:, it % 2, k, :],
                                           d_VN[:, k, h * P:(h + 1) * P], start=k == 0, stop=k == 3)
                        mm.then_inc(o_done, 1)

                    tp_first = tp
                    scores(0)
                    scores(1)
                    for it in range(2 * HEADS):
                        if it + 2 < 2 * HEADS:
                            scores(it + 2)
                        turn_p(it)
                        if it >= 1:
                            values(it - 1, tp_first + it - 1)
                    values(2 * HEADS - 1, tp_first + 2 * HEADS - 1)
                    its += 2 * HEADS
                    pe.wait_ge(o_taken, its)
                    pe.wait_ge(tp_taken, tp + 2)
                    pe.wait_ge(on_ready, 1)
                    for hh in range(HEADS // 2):
                        for h2 in range(2):
                            for t in range(TT):
                                mm = pe.transpose(PS[:, 4 + hh, (2 * h2 + t) * P:(2 * h2 + t + 1) * P],
                                                  d_ON[:, t, (2 * hh + h2) * P:(2 * hh + h2 + 1) * P], ident[:, :])
                        mm.then_inc(ot_done, 1)
                    linear(s["u0"] + 24, s["c0"], 8, 0, T, oh_ready, 0, 1)

                elif s["kind"] == "final":
                    norm(s, n)

                elif s["kind"] == "lru":
                    norm(s, n)
                    linear(s["u0"], s["c0"], 16, 0, T, h_ready, s["h0"], 1)
                    pe.wait_ge(psum_free, s["c0"] + 16 + RING)
                    for half in range(2):
                        u = s["u0"] + 16 + half
                        pe.wait_ge(lo_ready, RING + u + 1)
                        for c in range(DC):
                            pe.wait_ge(xc_lo, c + 1)
                            mm = block3(PS[:, 4 * half + c // 2, (c % 2) * T:(c % 2 + 1) * T], u % RING, c,
                                        H_hi[:, c, T:2 * T], H_lo[:, c, T:2 * T], True, True)
                        mm.then_inc(unit_done, 1)
                    linear(s["u0"] + 18, s["c0"] + 16, 8, 0, T, y_lo, 0, 1)

                elif s["kind"] == "dil":
                    norm(s, n)

                    def turn_group(g):
                        nonlocal tp
                        pe.wait_ge(kn_ready, 6 + g + 1)
                        blocks = [(h, t) for h in range(2 if g < 3 else 4) for t in range(TT)]
                        for b0 in range(0, len(blocks), 4):
                            pe.wait_ge(tp_taken, tp + 1)
                            for b, (h, t) in enumerate(blocks[b0:b0 + 4]):
                                mm = pe.transpose(PS[:, 4 + tp % 2, b * P:(b + 1) * P],
                                                  b_N[:, g % 2, t, h * P:(h + 1) * P], ident[:, :])
                            mm.then_inc(tp_done, 1)
                            tp += 1

                    for g in range(9):
                        project(s, g, TT, 2 * (g % 2), 0 if g < 3 else T,
                                {0: s["h0"] + DC, 3: s["h0"] + 2 * DC}.get(g))
                        if g:
                            turn_group(g - 1)
                    turn_group(8)
                    pe.wait_ge(tp_taken, tp + 2)
                    pe.wait_ge(proj_taken, s["p0"] + 9 + 2)

                    def scores(it):
                        h, qt = divmod(it, TT)
                        w = (qt + 1) * P
                        if it >= 2:
                            pe.wait_ge(nb_ready, its + it - 1)
                        for g in range(3):
                            at = (it % 2) * 1024 + g * w
                            mm = pe.matmul(PSf[:, at:at + w], b_QT[:, g * HEADS + h, qt * P:(qt + 1) * P],
                                           b_KT[:, 2 * g + h // 4, 0:w], start=True, stop=True)
                        mm.then_inc(s_done, 1)

                    def turn_p(it):
                        qt = it % TT
                        pe.wait_ge(a_ready, its + it + 1)
                        if it >= 2:
                            pe.wait_ge(o_taken, its + it - 1)
                        for b in range(3 * (qt + 1)):
                            at = 2048 + (it % 2) * 1024 + b * P
                            mm = pe.transpose(PSf[:, at:at + P], b_S[:, it % 2, b * P:(b + 1) * P], ident[:, :])
                        mm.then_inc(tp_done, 1)

                    def values(it):
                        h, qt = divmod(it, TT)
                        pe.wait_ge(tp_taken, tp + it + 3)
                        at = 2048 + (it % 2) * 1024 + 896
                        for g in range(3):
                            for k in range(qt + 1):
                                b = g * (qt + 1) + k
                                mm = pe.matmul(PSf[:, at:at + P], b_VN[:, k, g, (h // 4) * P:(h // 4 + 1) * P],
                                               b_PT[:, it % 2, b * P:(b + 1) * P],
                                               start=b == 0, stop=b == 3 * (qt + 1) - 1)
                        mm.then_inc(o_done, 1)

                    scores(0)
                    scores(1)
                    for it in range(2 * HEADS):
                        if it + 2 < 2 * HEADS:
                            scores(it + 2)
                        turn_p(it)
                        if it >= 1:
                            values(it - 1)
                    values(2 * HEADS - 1)
                    tp += 2 * HEADS
                    its += 2 * HEADS
                    pe.wait_ge(o_taken, its)
                    linear(s["u0"] + 36, s["c0"], 8, 0, T, o_taken, its - DC, 1)

        @block.scalar
        def _(act):
            act.sem_inc(tp_taken, 2)

            def split(base, i, stride, k):
                if isinstance(i, int) and base + stride * i + k >= TOTAL:
                    return
                slot = (base + k) % RING
                act.wait_ge(raw_ld[slot], 16 * (stride // RING) * i + 16 * ((base + k) // RING + 1))
                act.wait_ge(unit_done, stride * i + (base + k + 1))
                act.copy(W_hi[:, slot, :], raw[:, slot, :]).then_inc(hi_ready, 1)

            def split_units(s, first, n):
                def body(i):
                    for k in range(4):
                        split(s["u0"] + AHEAD + first, i, 4, k)
                loop(act, 0, n // 4, body)

            def norm(s, n):
                act.wait_ge(norm_pe, 2 * s["norm_i"] + 1)
                act.activation(std[:, 0:n // P], PS[:, SUM_BANK, 0:n // P], ACT.Sqrt, bias=EPS, scale=1.0 / D)\
                   .then_inc(norm_sd, 1)

            def high_parts(s, n, t0, shift, dst):
                for d in range(DC):
                    act.wait_ge(t_ready, t0 + d + 1)
                    for h, cols in halves(n):
                        if shift is None:
                            ins = act.copy(dst(d, cols), work[:, d % 2, cols])
                        else:
                            ins = act.activation(dst(d, cols), work[:, d % 2, cols], ACT.Identity,
                                                 bias=mods[:, shift, d, h:h + 1])
                    ins.then_inc(h_hi_ready, 1)

            act.wait_ge(in_vec, 16)
            act.wait_ge(start_ready, 1)
            act.activation(silu_c[:, :, 0:2], V("c").rearrange("p (d s) -> p d s", s=2), ACT.Silu)\
               .then_inc(silu_c_ready, 1)
            act.wait_ge(start_ready, 2)
            act.activation(sp_t[:, 1, :], sp_t[:, 0, :], ACT.Exp, scale=-1.0)
            act.activation(lam[:, 2:4], lam[:, 0:2], ACT.Exp).then_inc(start_act, 1)
            act.wait_ge(start_ready, 3)
            act.activation(trig[:, 3:5, :, :], trig[:, 1:3, :, :], ACT.Sin).then_inc(start_act, 1)
            norm(stages[0], 2 * T)
            for k in range(AHEAD):
                split(0, 0, 4, k)

            tp = its = 0
            for s in stages:
                n = s["n"]
                if s is not stages[0]:
                    norm(s, n)
                if s["kind"] == "ffn":
                    high_parts(s, n, s["t0"], s["mod"], lambda d, cols: H_hi[:, d, cols])

                    def body(i):
                        for k in range(4):
                            split(s["u0"] + AHEAD, i, 4, k)
                            if k % 2 == 0:
                                act.wait_ge(unit_done, RING + s["u0"] + 4 * i + (k + 1))
                                act.wait_ge(psum_free, s["c0"] + 4 * i + (k + 2))
                                act.activation(work[:, k // 2, 0:n], PS[:, (s["c0"] + k) % RING, 0:n], ACT.Silu)\
                                   .then_inc(silu_ready, 1)
                    loop(act, 0, FC // 2, body)

                    def body(i):
                        for k in range(12):
                            split(s["u0"] + 2 * FC + AHEAD, i, 12, k)
                    if s is stages[-1]:
                        body(0)
                        body(1)
                    else:
                        loop(act, 0, 2, body)

                elif s["kind"] == "pool":
                    high_parts(s, n, s["t0"], s["mod"],
                               lambda d, cols: pool_h[:, d, cols.start // T, PAD:PAD + T])
                    for d in range(DC):
                        act.wait_ge(t_ready, s["t0"] + DC + d + 1)
                        act.copy(H_hi[:, d, 0:n], work[:, d % 2, 0:n]).then_inc(h_hi_ready, 1)
                    for k in range(2):
                        split(s["u0"] + AHEAD, 0, 4, k)

                elif s["kind"] == "diff":
                    high_parts(s, n, s["t0"], s["mod"], lambda d, cols: H_hi[:, d, cols])
                    split_units(s, 0, 24)
                    for h in range(HEADS):
                        act.wait_ge(tp_done, tp + 1)
                        act.copy(d_KT[:, h, :], PS[:, 4 + tp % 2, :]).then_inc(tp_taken, 1)
                        tp += 1
                    for hh in range(HEADS // 2):
                        act.wait_ge(tp_done, tp + 1)
                        act.copy(d_QT[:, 2 * hh:2 * hh + 2, :],
                                 PS[:, 4 + tp % 2, :].rearrange("p (h t) -> p h t", h=2)).then_inc(tp_taken, 1)
                        tp += 1

                    def exps(it):
                        act.wait_ge(nb_ready, its + it + 1)
                        if it >= 2:
                            act.wait_ge(a_ready, its + it - 1)
                        for j in range(2):
                            at = 2 * (it % 2) + j
                            ins = act.activation(d_P[:, it % 2, j, :], PS[:, at, :], ACT.Exp,
                                                 bias=stat[:, 4 + at:5 + at], scale=DIFF_SCALE,
                                                 accum_out=stat[:, 8 + at:9 + at])
                        ins.then_inc(p_ready, 1)

                    def copy_p(it):
                        nonlocal tp
                        act.wait_ge(tp_done, tp + 1)
                        if it >= 2:
                            act.wait_ge(o_done, its + it - 1)
                        act.copy(d_AT[:, it % 2, :, :], PS[:, 4 + tp % 2, :].rearrange("p (k q) -> p k q", k=4))\
                           .then_inc(tp_taken, 1)
                        tp += 1

                    def take_o(it):
                        h, qt = divmod(it, TT)
                        act.wait_ge(o_done, its + it + 1)
                        act.copy(d_ON[:, qt, h * P:(h + 1) * P], PS[:, 6 + it % 2, 0:P])
                        if it >= 2:
                            act.wait_ge(o_taken, its + it - 1)
                        act.activation(work[:, it % 2, 0:P], PS[:, 6 + it % 2, 0:P], ACT.Square,
                                       accum_out=stat[:, 16 + it:17 + it]).then_inc(o_taken, 1)

                    exps(0)
                    for it in range(2 * HEADS):
                        if it + 1 < 2 * HEADS:
                            exps(it + 1)
                        copy_p(it)
                        if it >= 1:
                            take_o(it - 1)
                    take_o(2 * HEADS - 1)
                    its += 2 * HEADS
                    act.wait_ge(o_taken, its)
                    act.activation(stat[:, 32:48], stat[:, 16:32], ACT.Sqrt, bias=EPS, scale=1.0 / P)\
                       .then_inc(o_sd, 1)
                    for hh in range(HEADS // 2):
                        act.wait_ge(ot_done, hh + 1)
                        act.copy(H_hi[:, 2 * hh:2 * hh + 2, 0:T],
                                 PS[:, 4 + hh, :].rearrange("p (h t) -> p h t", h=2)).then_inc(oh_hi, 1)
                    split_units(s, 24, 8)

                elif s["kind"] == "lru":
                    high_parts(s, n, s["t0"], None, lambda d, cols: H_hi[:, d, cols])
                    for k in range(16):
                        split(s["u0"] + AHEAD, 0, 4, k)
                        if k < DC:
                            act.wait_ge(unit_done, RING + s["u0"] + k + 1)
                            act.activation(l_G[:, k, :], PS[:, (s["c0"] + k) % RING, 0:T], ACT.Gelu_apprx_tanh)\
                               .then_inc(gelu_done, 1)
                        else:
                            act.wait_ge(xc_ready, k - DC + 1)
                            act.copy(H_hi[:, k - DC, T:2 * T], l_XC[:, k - DC, :]).then_inc(xc_hi, 1)
                    for half, (dst, bias) in enumerate(((l_R, "ga_b"), (l_I, "gx_b"))):
                        split(s["u0"] + AHEAD, 0, 4, 16 + half)
                        act.wait_ge(unit_done, RING + s["u0"] + 16 + half + 1)
                        for c in range(DC):
                            act.activation(dst[:, c, :], PS[:, 4 * half + c // 2, (c % 2) * T:(c % 2 + 1) * T],
                                           ACT.Sigmoid, bias=V(bias)[:, c:c + 1]).then_inc(sig_done, 1)
                    act.wait_ge(sig_done, 2 * DC)
                    for c in range(DC):
                        act.activation(l_A[:, c, :], l_R[:, c, :], ACT.Exp, scale=nsp8[:, c:c + 1])
                        act.activation(l_T[:, c, :], l_R[:, c, :], ACT.Tanh, scale=sp8[:, c:c + 1]).then_inc(a_t_done, 1)
                    for q in range(4):
                        act.wait_ge(om_ready, q + 1)
                        act.activation(l_T[:, 2 * q:2 * q + 2, :], l_T[:, 2 * q:2 * q + 2, :], ACT.Sqrt)\
                           .then_inc(sqrt_done, 1)
                    for q in range(4):
                        act.wait_ge(y_ready, q + 1)
                        act.copy(H_hi[:, 2 * q:2 * q + 2, 0:T], l_H[:, 2 * q:2 * q + 2, :]).then_inc(y_hi, 1)
                    split_units(s, 18, 8)

                elif s["kind"] == "dil":
                    high_parts(s, n, s["t0"], None, lambda d, cols: H_hi[:, d, cols])
                    high_parts(s, n, s["t0"] + DC, None, lambda d, cols: H_hi[:, d, T:2 * T])

                    def copy_group(g):
                        nonlocal tp
                        for b in range(1 if g < 3 else 2):
                            act.wait_ge(tp_done, tp + 1)
                            h = 4 * (g - 3) + 2 * b
                            dst = b_KT[:, 2 * g:2 * g + 2, :] if g < 3 else b_QT[:, h:h + 2, :]
                            act.copy(dst, PS[:, 4 + tp % 2, :].rearrange("p (h t) -> p h t", h=2)).then_inc(tp_taken, 1)
                            tp += 1

                    for g in range(9):
                        split_units(s, 4 * g, 4)
                        heads = 2 if g < 3 else 4
                        act.wait_ge(unit_done, RING + s["u0"] + 4 * g + 4)
                        if g:
                            act.wait_ge(ss_ready, g)
                        for t in range(TT):
                            ins = act.activation(work[:, t, 0:heads * P], PS[:, 2 * (g % 2) + t, 0:heads * P], ACT.Square)
                        ins.then_inc(sq_done, 1)
                        act.wait_ge(ss_ready, g + 1)
                        act.activation(stat[:, 8:8 + TT * heads], stat[:, 0:TT * heads], ACT.Sqrt, bias=EPS, scale=1.0 / P)\
                           .then_inc(sd_done, 1)
                        if g:
                            copy_group(g - 1)
                    copy_group(8)

                    def exps(it):
                        w = 3 * (it % TT + 1) * P
                        act.wait_ge(nb_ready, its + it + 1)
                        act.activation(b_S[:, it % 2, 0:w], b_S[:, it % 2, 0:w], ACT.Exp,
                                       bias=stat[:, 32 + it % 2:33 + it % 2],
                                       accum_out=stat[:, 34 + it % 2:35 + it % 2]).then_inc(p_ready, 1)

                    def copy_p(it):
                        w = 3 * (it % TT + 1) * P
                        at = 2048 + (it % 2) * 1024
                        act.wait_ge(tp_done, tp + it + 1)
                        if it >= 2:
                            act.wait_ge(o_done, its + it - 1)
                        act.copy(b_PT[:, it % 2, 0:w], PSf[:, at:at + w]).then_inc(tp_taken, 1)

                    def take_o(it):
                        h, qt = divmod(it, TT)
                        act.wait_ge(o_done, its + it + 1)
                        act.copy(H_hi[:, h, qt * P:(qt + 1) * P],
                                 PSf[:, (it % 2) * 1024 + 2944:(it % 2) * 1024 + 3072]).then_inc(o_hi, 1)

                    exps(0)
                    for it in range(2 * HEADS):
                        if it + 1 < 2 * HEADS:
                            exps(it + 1)
                        copy_p(it)
                        if it >= 1:
                            take_o(it - 1)
                    take_o(2 * HEADS - 1)
                    tp += 2 * HEADS
                    its += 2 * HEADS
                    split_units(s, 36, 8)

        @block.vector
        def _(ve):
            own = Tally(ve, vself)
            ve.sem_inc(lo_ready, RING)
            ve.sem_inc(psum_free, RING)
            ve.sem_inc(proj_taken, 2)
            ve.sem_inc(gu_ready, 1)

            def step(ins):
                own.mark(ins)
                own.sync()

            def split(base, i, stride, k):
                if isinstance(i, int) and base + stride * i + k >= TOTAL:
                    return
                slot = (base + k) % RING
                ve.wait_ge(hi_ready, stride * i + (base + k + 1))
                ve.tensor_tensor(W_lo[:, slot, :], raw[:, slot, :], W_hi[:, slot, :], ALU.subtract).then_inc(lo_ready, 1)

            def split_units(s, first, n):
                def body(i):
                    for k in range(4):
                        split(s["u0"] + AHEAD + first, i, 4, k)
                own.loop(0, n // 4, 0, body)

            def take_mod(m):
                if isinstance(m, int) and m < MODS_FIRST:
                    ve.wait_ge(first_used, 8 * m + 8)
                else:
                    ve.wait_ge(ada_used, (m - MODS_FIRST) * 8 + 10)
                step(ve.transpose(ada_T[:, :, :], PS[:, ADA_BANK, 0:256].rearrange("p (b c) -> p b c", c=32)))
                ve.sem_inc(ada_taken, 1)
                for h in range(2):
                    ins = ve.tensor_tensor(mods[:, m, :, h], ada_T[:, :, h],
                                           V("ada_b")[:, bass.ds(m * DC, DC)], ALU.add)
                step(ins)

            def add_square(q, d, n):
                if not isinstance(q, int) or q:
                    ve.wait_ge(ssq_ready, q)
                step(ve.tensor_tensor(work[:, 2, 0:n], X[:, d, 0:n], X[:, d, 0:n], ALU.mult))
                ve.tensor_tensor(ssq[:, 0:n], ssq[:, 0:n], work[:, 2, 0:n], ALU.add).then_inc(ssq_ready, 1)

            def gains(s):
                if s.get("mod") is not None:
                    own.sync()
                    j = s["mod"] + 1
                    g = V("norm_g")[:, (s["mod"] // 3) * DC:(s["mod"] // 3 + 1) * DC]
                    for h in range(2):
                        ins = ve.scalar_tensor_tensor(gain[:, :, h], mods[:, j, :, h], 1.0, g, ALU.add, ALU.mult)
                    own.mark(ins)

            def norm(s, n):
                ve.wait_ge(norm_sd, s["norm_i"] + 1)
                ve.reciprocal(rstd[:, 0:n // P], std[:, 0:n // P]).then_inc(norm_rs, 1)
                ve.wait_ge(norm_pe, 2 * s["norm_i"] + 2)
                step(ve.memset(ssq[:, :], 0.0))

            def set_gate(s, scale=None):
                m = s["mod"] + 2
                for h in range(2):
                    if scale is None:
                        ins = ve.tensor_scalar(gate[:, :, h], mods[:, m, :, h], 0.5 if s["kind"] == "ffn" else 1.0,
                                               None, ALU.mult)
                    else:
                        ins = ve.tensor_tensor(gate[:, :, h], mods[:, m, :, h], scale, ALU.mult)
                step(ins)

            def normed(n, d, factor):
                for h, cols in halves(n):
                    ins = ve.scalar_tensor_tensor(work[:, d % 2, cols], X[:, d, cols], factor(d, h),
                                                  PS[:, BC_BANK, cols], ALU.mult, ALU.mult)
                ins.then_inc(t_ready, 1)

            def h_chunks(s, n, t0, h0, shift, factor, lo=0):
                if h0:
                    ve.wait_ge(h_ready, h0)
                normed(n, 0, factor)
                for d in range(DC):
                    if d + 1 < DC:
                        if h0 + d:
                            ve.wait_ge(h_ready, h0 + d)
                        normed(n, d + 1, factor)
                    ve.wait_ge(h_hi_ready, t0 + d + 1)
                    for h, cols in halves(n):
                        to = slice(lo + cols.start, lo + cols.stop)
                        high = H_hi[:, d, to].bitcast(F32)
                        if shift is None:
                            ins = ve.tensor_tensor(H_lo[:, d, to], work[:, d % 2, cols], high, ALU.subtract)
                        else:
                            ins = ve.scalar_tensor_tensor(H_lo[:, d, to], work[:, d % 2, cols],
                                                          mods[:, shift, d, h:h + 1], high, ALU.add, ALU.subtract)
                    ins.then_inc(h_ready, 1)

            def residual(s, n, c, bank, d, u, squares=True):
                ve.wait_ge(unit_done, u + (RING + 1))
                for h, cols in halves(n):
                    if s.get("mod") is None:
                        ins = ve.tensor_tensor(X[:, d, cols], PS[:, bank, cols], X[:, d, cols], ALU.add)
                    else:
                        ins = ve.scalar_tensor_tensor(X[:, d, cols], PS[:, bank, cols], gate[:, d, h:h + 1],
                                                      X[:, d, cols], ALU.mult, ALU.add)
                ins.then_inc(psum_free, 1)
                if squares:
                    ve.wait_ge(psum_free, c + (RING + 1))
                    add_square(DC * (s["norm_i"] + 1) + d, d, n)

            def linear_out(s, u_off, c_off, n):
                squares = s is not stages[-1]

                def body(i):
                    for k in range(4):
                        split(s["u0"] + AHEAD + u_off, i, 4, k)
                        residual(s, n, s["c0"] + c_off + 4 * i + k, (s["c0"] + c_off + k) % RING,
                                 4 * i + k, s["u0"] + u_off + 4 * i + k, squares)
                own.loop(0, 2, 4 if squares else 0, body)

            ve.memset(ones[:, :], 1.0)
            ve.memset(ssq[:, :], 0.0)
            ve.memset(silu_c[:, :, :], 0.0).then_inc(start_ready, 1)
            ve.wait_ge(in_vec, 16)
            ve.scalar_tensor_tensor(sp_t[:, 0, :], V("lam"), -1.0, V("lam"), ALU.mult, ALU.max)
            dl = V("diff_lam").rearrange("p (a b d) -> p a b d", a=2, b=2)
            step(ve.tensor_tensor(dots[:, :, :], dl[:, :, 0, :], dl[:, :, 1, :], ALU.mult))
            ve.tensor_reduce(lam[:, 0:2], dots[:, :, :], AX.X, ALU.add)\
              .then_inc(start_ready, 1)
            ve.wait_ge(in_pos, 32)
            step(ve.tensor_copy(posf[:, :], pos[:, :]))
            ang, r, cr = trig[:, 0, :, :], trig[:, 1, :, :], trig[:, 2, :, :]
            for t in range(TT):
                ins = ve.tensor_scalar(trig[:, 0, t, :], inv_freq[:, :], posf[:, t:t + 1], None, ALU.mult)
            step(ins)
            magic = 1.5 * 2.0 ** 23
            step(ve.tensor_scalar(cr, ang, 1.0 / (2 * math.pi), magic, ALU.mult, ALU.add))
            step(ve.tensor_scalar(cr, cr, magic, None, ALU.subtract))
            left = 2 * math.pi
            for n_bits in (6, 17, 30):
                part = math.floor(left * 2.0 ** n_bits) / 2.0 ** n_bits
                left -= part
                step(ve.scalar_tensor_tensor(r if n_bits == 30 else ang, cr, -part, ang, ALU.mult, ALU.add))
            step(ve.tensor_scalar(r, r, 3.1415925, -3.1415925, ALU.min, ALU.max))
            step(ve.scalar_tensor_tensor(cr, r, -1.0, r, ALU.mult, ALU.max))
            ve.tensor_scalar(cr, cr, -1.0, math.pi / 2, ALU.mult, ALU.add).then_inc(start_ready, 1)
            ve.wait_ge(start_act, 1)
            e, w, w2, acc = (sp_t[:, k, :] for k in (1, 2, 3, 0))
            step(ve.tensor_scalar(w, e, 2.0, None, ALU.add))
            step(ve.reciprocal(w, w))
            step(ve.tensor_tensor(w, w, e, ALU.mult))
            step(ve.tensor_tensor(w2, w, w, ALU.mult))
            step(ve.tensor_scalar(acc, w2, 1.0 / 17, None, ALU.mult))
            for k in range(15, 1, -2):
                step(ve.scalar_tensor_tensor(acc, acc, 1.0 / k, w2, ALU.add, ALU.mult))
            step(ve.scalar_tensor_tensor(w, acc, 1.0, w, ALU.add, ALU.mult))
            step(ve.tensor_scalar(w2, V("lam"), -8.0, 0.0, ALU.mult, ALU.max))
            step(ve.scalar_tensor_tensor(sp8[:, :], w, 16.0, w2, ALU.mult, ALU.add))
            ve.tensor_scalar(nsp8[:, :], sp8[:, :], -1.0, None, ALU.mult)
            step(ve.tensor_tensor(lam[:, 0:1], lam[:, 3:4], lam[:, 2:3], ALU.subtract))
            ve.tensor_scalar(lam[:, 0:1], lam[:, 0:1], LAM_INIT, None, ALU.subtract)
            ve.wait_ge(start_act, 2)
            for h in range(2):
                ve.tensor_copy(b_cos[:, :, 16 * h:16 * h + 16], trig[:, 4, :, :])
                ins = ve.tensor_scalar(b_sin[:, :, 16 * h:16 * h + 16], trig[:, 3, :, :], -1.0 if h == 0 else 1.0,
                                       None, ALU.mult)
            step(ins)
            ve.wait_ge(in_x, 16)
            for d in range(DC):
                add_square(d, d, 2 * T)
            norm(stages[0], 2 * T)
            for m in range(MODS_FIRST):
                take_mod(m)
            gains(stages[0])
            own.sync()
            for k in range(AHEAD):
                split(0, 0, 4, k)

            tp = its = regions = 0
            for s in stages:
                n, last = s["n"], s is stages[-1]
                factor = (lambda d, h: gain[:, d, h:h + 1]) if s.get("mod") is not None else \
                    (lambda d, h: V(s["gain"])[:, d:d + 1])
                if s["kind"] in ("pool", "diff", "dil"):
                    ve.sem_inc(region_free, 1)
                if s is not stages[0]:
                    gains(s)
                    norm(s, n)

                if s["kind"] == "ffn":
                    h_chunks(s, n, s["t0"], s["h0"], s["mod"], factor)

                    def pair(i, k):
                        ve.wait_ge(silu_ready, s["f0"] + 2 * i + (k + 1))
                        ve.wait_ge(unit_done, RING + s["u0"] + 4 * i + (2 * k + 2))
                        m = work[:, 2, 0:n]
                        ve.wait_ge(gu_ready, s["f0"] + 2 * i + (k + 1))
                        ve.tensor_tensor(m, work[:, k, 0:n], PS[:, (s["c0"] + 2 * k + 1) % RING, 0:n], ALU.mult)\
                          .then_inc(psum_free, 2)
                        ve.wait_ge(psum_free, RING + s["c0"] + 4 * i + (2 * k + 2))
                        step(ve.tensor_copy(G_hi[:, 2 * i + k, 0:n], m))
                        ve.tensor_tensor(G_lo[:, 2 * i + k, 0:n], m, G_hi[:, 2 * i + k, 0:n], ALU.subtract)\
                          .then_inc(gu_ready, 1)

                    def body(i, with_ada=False):
                        for k in range(4):
                            split(s["u0"] + AHEAD, i, 4, k)
                            if k % 2:
                                pair(i, k // 2)
                        if with_ada:
                            take_mod(s["ada"][0] + i)
                    n_ada = s["ada"][1] - s["ada"][0] if s["ada"] else 0
                    if n_ada:
                        own.loop(0, n_ada, 4, lambda i: body(i, True))
                    if n_ada < FC // 2:
                        own.loop(n_ada, FC // 2, 2, body)
                    own.sync()
                    if s["mod"] is not None:
                        set_gate(s)

                    def body(i):
                        for k in range(4):
                            for part in range(3):
                                split(s["u0"] + 2 * FC + AHEAD, i, 12, 3 * k + part)
                            c1 = s["c0"] + 2 * FC
                            residual(s, n, c1 + 4 * i + k, (c1 + k) % RING, 4 * i + k,
                                     s["u0"] + 2 * FC + 12 * i + 3 * k + 2, not last)
                    if last:
                        body(0)
                        body(1)
                    else:
                        own.loop(0, 2, 4, body)

                elif s["kind"] == "pool":
                    for at in (0, PAD + T):
                        ins = ve.memset(pool_h[:, :, :, at:at + PAD], 0.0)
                    step(ins)
                    set_gate(s, V("pool_scale"))
                    normed(n, 0, factor)
                    for d in range(1, DC + 1):
                        if d >= 2:
                            ve.wait_ge(h_hi_ready, s["t0"] + d - 1)
                        if d < DC:
                            normed(n, d, factor)
                    ve.wait_ge(stage_ld, 16)
                    for g in range(4):
                        ve.wait_ge(h_hi_ready, s["t0"] + DC)
                        src = pool_h[:, 2 * g:2 * g + 2, :, :]
                        lo, hi = 0, T + 2 * PAD
                        for k in range(g + 1):
                            a_, b_ = (1, 0) if k == 0 else (1 << (k - 1), 1 << (k - 1))
                            dst = pool_s[:, k % 2, :, :, :]
                            lo2, hi2 = lo + a_, hi - b_
                            step(ve.tensor_tensor(dst[:, :, :, lo2:hi2], src[:, :, :, lo2 - a_:hi2 - a_],
                                                  src[:, :, :, lo2 + b_:hi2 + b_], ALU.add))
                            src, lo, hi = dst, lo2, hi2
                        for k in range(2):
                            d = 2 * g + k
                            o = work[:, d % 2, :].rearrange("p (s t) -> p s t", s=2)
                            if d >= 2:
                                ve.wait_ge(h_hi_ready, s["t0"] + DC + d - 1)
                            cnt = pool_n[:, g, :].unsqueeze(1).to_broadcast([P, 2, T])
                            step(ve.tensor_tensor(o, src[:, k, :, PAD:PAD + T], cnt, ALU.mult))
                            own.mark(ve.tensor_tensor(o, o, pool_h[:, d, :, PAD:PAD + T], ALU.subtract))
                            own.sync()
                            ve.sem_inc(t_ready, 1)
                        for k in range(2):
                            d = 2 * g + k
                            ve.wait_ge(h_hi_ready, s["t0"] + DC + d + 1)
                            ve.tensor_tensor(H_lo[:, d, 0:n], work[:, d % 2, 0:n], H_hi[:, d, 0:n], ALU.subtract)\
                              .then_inc(h_ready, 1)
                    for half in range(2):
                        split(s["u0"] + AHEAD, 0, 4, half)
                        for k in range(4):
                            d = 4 * half + k
                            residual(s, n, s["c0"] + d, (s["c0"] + d) % RING, d, s["u0"] + half, not last)

                elif s["kind"] == "diff":
                    h_chunks(s, n, s["t0"], s["h0"], s["mod"], factor)
                    ve.wait_ge(stage_ld, 64)
                    ve.tensor_scalar(d_g[:, :], d_g[:, :], 1.0 - LAM_INIT, None, ALU.mult)
                    set_gate(s)

                    def rope(bank, dst, t):
                        src = PS[:, bank, :].rearrange("p (x c) -> p x c", c=64)
                        o0 = work[:, 0, :].rearrange("p (x c) -> p x c", c=64)
                        ve.tensor_tensor(o0, src, d_cos[:, t, :].unsqueeze(1).to_broadcast([P, 8, 64]), ALU.mult)
                        for half in range(2):
                            o1 = work[:, 1, :].rearrange("p (x a c) -> p x a c", a=2, c=32)[:, :, :, 16 * half:16 * half + 16]
                            other = PS[:, bank, :].rearrange("p (x a c) -> p x a c", a=2, c=32)[:, :, :, 16 - 16 * half:32 - 16 * half]
                            sn = d_sin[:, t, :].rearrange("p (a c) -> p a c", c=32)[:, :, 16 * half:16 * half + 16]
                            ins = ve.tensor_tensor(o1, other, sn.unsqueeze(1).to_broadcast([P, 8, 2, 16]), ALU.mult)
                        step(ins)
                        return ve.tensor_tensor(dst, work[:, 0, :], work[:, 1, :], ALU.add)

                    for g in range(6):
                        for q in range(4):
                            split(s["u0"] + AHEAD, 0, 4, 4 * g + q)
                        ve.wait_ge(unit_done, RING + s["u0"] + 4 * g + 4)
                        cols = slice((g % 2) * 512, (g % 2) * 512 + 512)
                        bank = 4 * (g % 2)
                        dst = (d_KN, d_VN, d_QN)[g // 2]
                        plain = {0: (2, 3), 1: (0, 1, 2, 3), 2: ()}[g // 2]
                        for t in plain:
                            ins = ve.tensor_copy(dst[:, t, cols], PS[:, bank + t, :])
                        if g // 2 != 1:
                            for t in range(TT):
                                ins = rope(bank + t, dst[:, t, cols], t)
                                if t < TT - 1:
                                    step(ins)
                        ins.then_inc(kn_ready, 1)
                        ve.wait_ge(kn_ready, g + 1)
                        ve.sem_inc(proj_taken, 1)

                    tp += HEADS + HEADS // 2

                    def maxima(it):
                        at = 2 * (it % 2)
                        ve.wait_ge(s_done, its + it + 1)
                        step(ve.tensor_reduce(stat[:, at:at + 2], PS[:, at:at + 2, :], AX.X, ALU.max))
                        ve.tensor_scalar(stat[:, 4 + at:6 + at], stat[:, at:at + 2], -DIFF_SCALE, None, ALU.mult)\
                          .then_inc(nb_ready, 1)

                    def weights(it):
                        at = 2 * (it % 2)
                        ve.wait_ge(p_ready, its + it + 1)
                        step(ve.reciprocal(stat[:, 12 + at:14 + at], stat[:, 8 + at:10 + at]))
                        step(ve.tensor_scalar(d_P[:, it % 2, 1, :], d_P[:, it % 2, 1, :], stat[:, 13 + at:14 + at],
                                              lam[:, 0:1], ALU.mult, ALU.mult))
                        if it >= 2:
                            ve.wait_ge(tp_done, tp + it - 1)
                        ve.scalar_tensor_tensor(d_A[:, it % 2, :], d_P[:, it % 2, 0, :], stat[:, 12 + at:13 + at],
                                                d_P[:, it % 2, 1, :], ALU.mult, ALU.add).then_inc(a_ready, 1)

                    maxima(0)
                    for it in range(2 * HEADS):
                        if it + 1 < 2 * HEADS:
                            maxima(it + 1)
                        weights(it)
                    tp += 2 * HEADS
                    its += 2 * HEADS
                    ve.wait_ge(o_sd, 1)
                    step(ve.reciprocal(stat[:, 48:64], stat[:, 32:48]))
                    for it in range(2 * HEADS):
                        h, qt = divmod(it, TT)
                        o = d_ON[:, qt, h * P:(h + 1) * P]
                        ins = ve.scalar_tensor_tensor(o, o, stat[:, 48 + it:49 + it], d_g[:, :], ALU.mult, ALU.mult)
                    ins.then_inc(on_ready, 1)
                    for hh in range(HEADS // 2):
                        ve.wait_ge(oh_hi, hh + 1)
                        ve.tensor_tensor(H_lo[:, 2 * hh:2 * hh + 2, 0:T],
                                         PS[:, 4 + hh, :].rearrange("p (h t) -> p h t", h=2),
                                         H_hi[:, 2 * hh:2 * hh + 2, 0:T], ALU.subtract).then_inc(oh_ready, 2)
                    linear_out(s, 24, 0, T)

                elif s["kind"] == "final":
                    for d in range(DC):
                        step(ve.scalar_tensor_tensor(X[:, d, 0:T], X[:, d, 0:T], V("final_g")[:, d:d + 1],
                                                     PS[:, BC_BANK, 0:T], ALU.mult, ALU.mult))
                        add_square(DC * (s["norm_i"] + 1) + d, d, T)

                elif s["kind"] == "lru":
                    ve.memset(l_XB[:, :, 0:3], 0.0)
                    h_chunks(s, n, s["t0"], s["h0"], None, lambda d, h: V("a_norm")[:, d:d + 1])
                    for k in range(16):
                        split(s["u0"] + AHEAD, 0, 4, k)
                        if k < DC:
                            ve.wait_ge(gelu_done, k + 1)
                            ve.sem_inc(psum_free, 1)
                            continue
                        d = k - DC
                        c = s["c0"] + k
                        ve.wait_ge(unit_done, RING + s["u0"] + k + 1)
                        ve.tensor_copy(l_XB[:, d, 3:T + 3], PS[:, c % RING, 0:T]).then_inc(psum_free, 1)
                        ve.wait_ge(psum_free, RING + c + 1)
                        cw = V("conv_w").rearrange("p (k d) -> p k d", k=4)
                        step(ve.tensor_scalar(l_XC[:, d, :], l_XB[:, d, 0:T], cw[:, 0, d:d + 1],
                                              V("conv_b")[:, d:d + 1], ALU.mult, ALU.add))
                        for j in range(1, 4):
                            ins = ve.scalar_tensor_tensor(l_XC[:, d, :], l_XB[:, d, j:j + T], cw[:, j, d:d + 1],
                                                          l_XC[:, d, :], ALU.mult, ALU.add)
                            if j < 3:
                                step(ins)
                        ins.then_inc(xc_ready, 1)
                        ve.wait_ge(xc_hi, d + 1)
                        ve.tensor_tensor(H_lo[:, d, T:2 * T], l_XC[:, d, :], H_hi[:, d, T:2 * T], ALU.subtract)\
                          .then_inc(xc_lo, 1)
                    for half in range(2):
                        split(s["u0"] + AHEAD, 0, 4, 16 + half)
                    for q in range(4):
                        two = slice(2 * q, 2 * q + 2)
                        ve.wait_ge(a_t_done, 2 * q + 2)
                        step(ve.tensor_tensor(l_H[:, two, :], l_A[:, two, :], l_A[:, two, :], ALU.mult))
                        for d in (2 * q, 2 * q + 1):
                            ins = ve.scalar_tensor_tensor(l_T[:, d, :], l_H[:, d, :], 1.0, l_T[:, d, :], ALU.add, ALU.mult)
                        ins.then_inc(om_ready, 1)
                        own.mark(ve.tensor_tensor(l_I[:, two, :], l_I[:, two, :], l_XC[:, two, :], ALU.mult))
                    for q in range(4):
                        two = slice(2 * q, 2 * q + 2)
                        ve.wait_ge(sqrt_done, q + 1)
                        step(ve.tensor_tensor(l_T[:, two, :], l_T[:, two, :], l_I[:, two, :], ALU.mult))
                        for d in (2 * q, 2 * q + 1):
                            ins = ve.tensor_tensor_scan(l_H[:, d, :], l_A[:, d, :], l_T[:, d, :], 0.0, ALU.mult, ALU.add)
                        step(ins)
                        ve.tensor_tensor(l_H[:, two, :], l_H[:, two, :], l_G[:, two, :], ALU.mult).then_inc(y_ready, 1)
                    for q in range(4):
                        two = slice(2 * q, 2 * q + 2)
                        ve.wait_ge(y_hi, q + 1)
                        ve.tensor_tensor(H_lo[:, two, 0:T], l_H[:, two, :], H_hi[:, two, 0:T], ALU.subtract)\
                          .then_inc(y_lo, 2)
                    linear_out(s, 18, 16, T)

                elif s["kind"] == "dil":
                    h_chunks(s, n, s["t0"], s["h0"], None, lambda d, h: V("kv_norm")[:, d:d + 1])
                    h_chunks(s, n, s["t0"] + DC, s["h0"] + DC, None, lambda d, h: V("b_norm")[:, d:d + 1], T)
                    ve.wait_ge(stage_ld, 16 * 7)
                    for g in range(9):
                        split_units(s, 4 * g, 4)
                        heads = 2 if g < 3 else 4
                        w = heads * P
                        bank = 2 * (g % 2)
                        ve.wait_ge(sq_done, g + 1)
                        ve.tensor_reduce(stat[:, 0:TT * heads],
                                         work[:, 0:TT, 0:w].rearrange("p t (h c) -> p t h c", c=P), AX.X, ALU.add)\
                          .then_inc(ss_ready, 1)
                        ve.wait_ge(sd_done, g + 1)
                        step(ve.reciprocal(stat[:, 16:16 + TT * heads], stat[:, 8:8 + TT * heads]))
                        if g >= 2:
                            ve.wait_ge(tp_done, tp + (g - 1 if g < 5 else 3 + 2 * (g - 4)))
                        table = b_gk[:, g, :] if g < 3 else b_gq[:, (g - 3) // 2, :]
                        for t in range(TT):
                            for h in range(heads):
                                at = 16 + t * heads + h
                                ins = ve.scalar_tensor_tensor(b_N[:, g % 2, t, h * P:(h + 1) * P],
                                                              PS[:, bank + t, h * P:(h + 1) * P], stat[:, at:at + 1],
                                                              table, ALU.mult, ALU.mult)
                        if g < 3:
                            ins = ve.tensor_copy(b_VN[:, :, g, :], PS[:, bank:bank + 2, w:2 * w])
                        step(ins)
                        ve.sem_inc(proj_taken, 1)
                        y = b_N[:, g % 2, :, 0:w].rearrange("p t (h c) -> p t h c", c=P)
                        ve.wait_ge(kn_ready, 6 + g)
                        for half in range(2):
                            sn = b_sin[:, :, 16 * half:16 * half + 16].unsqueeze(2).to_broadcast([P, TT, heads, 16])
                            ve.tensor_tensor(b_rb[:, :, 0:heads, 16 * half:16 * half + 16],
                                             y[:, :, :, 16 - 16 * half:32 - 16 * half], sn, ALU.mult)
                        step(ve.tensor_tensor(b_ra[:, :, 0:heads, :], y[:, :, :, 0:32],
                                              b_cos[:, :, :].unsqueeze(2).to_broadcast([P, TT, heads, 32]), ALU.mult))
                        ve.tensor_tensor(y[:, :, :, 0:32], b_ra[:, :, 0:heads, :], b_rb[:, :, 0:heads, :], ALU.add)\
                          .then_inc(kn_ready, 1)
                    tp += 15

                    def maxima(it):
                        qt, b = it % TT, it % 2
                        w = 3 * (qt + 1) * P
                        ve.wait_ge(s_done, its + it + 1)
                        if it >= 2:
                            ve.wait_ge(tp_done, tp + it - 1)
                        step(ve.scalar_tensor_tensor(b_S[:, b, 0:w], PSf[:, b * 1024:b * 1024 + w], DIL_SCALE,
                                                     b_mask[:, qt, 0:w], ALU.mult, ALU.add))
                        step(ve.tensor_reduce(stat[:, 36 + b:37 + b], b_S[:, b, 0:w], AX.X, ALU.max))
                        ve.tensor_scalar(stat[:, 32 + b:33 + b], stat[:, 36 + b:37 + b], -1.0, None, ALU.mult)\
                          .then_inc(nb_ready, 1)

                    def weights(it):
                        b = it % 2
                        w = 3 * (it % TT + 1) * P
                        ve.wait_ge(p_ready, its + it + 1)
                        step(ve.reciprocal(stat[:, 38 + b:39 + b], stat[:, 34 + b:35 + b]))
                        ve.tensor_scalar(b_S[:, b, 0:w], b_S[:, b, 0:w], stat[:, 38 + b:39 + b], None, ALU.mult)\
                          .then_inc(a_ready, 1)

                    def low_o(it):
                        h, qt = divmod(it, TT)
                        rows = slice(qt * P, (qt + 1) * P)
                        ve.wait_ge(o_hi, it + 1)
                        ve.tensor_tensor(H_lo[:, h, rows], PSf[:, (it % 2) * 1024 + 2944:(it % 2) * 1024 + 3072],
                                         H_hi[:, h, rows], ALU.subtract).then_inc(o_taken, 1)

                    maxima(0)
                    for it in range(2 * HEADS):
                        if it + 1 < 2 * HEADS:
                            maxima(it + 1)
                        weights(it)
                        if it >= 1:
                            low_o(it - 1)
                    low_o(2 * HEADS - 1)
                    tp += 2 * HEADS
                    its += 2 * HEADS
                    linear_out(s, 36, 0, T)


def chunks(w):
    k, m = w.shape[0] // P, w.shape[1] // P
    return w.reshape(k, P, m, P).transpose(2, 1, 0, 3).reshape(m, P, k * P)


def wide(w):
    n = w.shape[1] // 512
    return w.reshape(4, 2, P, n, 512).transpose(3, 0, 2, 1, 4).reshape(4 * n, P, 1024)


def ffn_units(w_in, w_out):
    g_u = chunks(w_in).reshape(2, FC, P, D).transpose(1, 0, 2, 3).reshape(2 * FC, P, D)
    w = w_out.reshape(FC, P, DC, P).transpose(2, 1, 0, 3)
    outs = np.zeros((DC, 3, P, D), w_out.dtype)
    at = 0
    for part, blocks in enumerate(W_OUT_PARTS):
        outs[:, part, :, 0:blocks * P] = w[:, :, at:at + blocks].reshape(DC, P, blocks * P)
        at += blocks
    return [g_u, outs.reshape(3 * DC, P, D)]


def column(v):
    return v.reshape(-1, P).T


def constants():
    n = np.arange(T)
    pool = np.zeros((4, T), np.float32)
    for g, win in enumerate((2, 4, 8, 16)):
        lo = np.clip(n - win // 2, 0, T - 1)
        hi = np.clip(n - win // 2 + win - 1, 0, T - 1)
        pool[g] = 1.0 / (hi - lo + 1)
    inv = (np.float32(10000.0) ** (-np.arange(0, 32, 2, dtype=np.float32) / np.float32(32))).astype(np.float32)
    ang = np.stack([(n // 64).astype(np.float32)[:, None] * inv, (n % 64).astype(np.float32)[:, None] * inv], 1)
    cos = np.concatenate([np.cos(ang), np.cos(ang)], -1).reshape(T, 64)
    sin = np.concatenate([-np.sin(ang), np.sin(ang)], -1).reshape(T, 64)
    q, k = n[:, None], n[None, :]
    allowed = [(q >= k) & ((q - k) % d == 0) & ((q - k) // d <= P) for d in (1, 4, 16)]
    mask = np.full((P, TT, 768), NEG, np.float32)
    for t in range(TT):
        w = (t + 1) * P
        for g in range(3):
            mask[:, t, g * w:(g + 1) * w] = np.where(allowed[g][t * P:(t + 1) * P, 0:w], 0.0, NEG)
    inv2 = (np.float32(500000.0) ** (-np.arange(0, 32, 2, dtype=np.float32) / np.float32(32))).astype(np.float32)
    tiles = lambda v: np.ascontiguousarray(v.astype(np.float32).reshape(TT, P, -1).transpose(1, 0, 2))
    return dict(ident=np.eye(P, dtype=np.float32), pool_n=np.ascontiguousarray(np.broadcast_to(pool, (P, 4, T))),
                d_cos=tiles(cos), d_sin=tiles(sin), mask=mask,
                inv_freq=np.ascontiguousarray(np.broadcast_to(inv2, (P, 16))))


def lay_out(i):
    w = []
    fi, fo = i["ffn_w_in"], i["ffn_w_out"]
    w += ffn_units(fi[0, 0], fo[0, 0])
    pw = i["pool_w"][0].reshape(4, 2, P, 2, P).transpose(0, 3, 1, 2, 4)
    w += [pw.reshape(2, 8, P, P).transpose(0, 2, 1, 3).reshape(2, P, D)]
    w += ffn_units(fi[0, 1], fo[0, 1])
    w += ffn_units(fi[1, 0], fo[1, 0])
    qkv = i["diff_w_qkv"][0]
    w += [wide(qkv[:, D:2 * D]), wide(qkv[:, 2 * D:]), wide(qkv[:, 0:D]), chunks(i["diff_w_o"][0])]
    w += ffn_units(fi[1, 1], fo[1, 1])
    w += [chunks(i["a_w_in_2"][0])]
    w += [i[name][0].transpose(1, 0, 2).reshape(1, P, D) for name in ("a_gate_a_w_2", "a_gate_x_w_2")]
    w += [chunks(i["a_w_out_2"][0])]
    w += ffn_units(i["a_ffn_w_in_2"][0], i["a_ffn_w_out_2"][0])
    w += [wide(i["w_kv_2"]), wide(i["b_w_q_2"][0]), chunks(i["b_w_o_2"][0])]
    w += ffn_units(i["b_ffn_w_in_2"][0], i["b_ffn_w_out_2"][0])
    ada = i["ada_w"].reshape(2, DC, P, 9, DC, 4, 32).transpose(0, 3, 1, 2, 5, 4, 6)
    vecs = dict(
        c=np.stack([i["c"][0], i["c_ctx"]], -1).reshape(DC, P, 2).transpose(1, 0, 2).reshape(P, 16),
        ada_b=column(i["ada_b"]), norm_g=column(i["norm_g"]), pool_scale=column(i["pool_scale"]),
        final_g=column(i["final_g"]), a_norm=column(i["a_norm_2"]), conv_w=column(i["a_conv_w_2"]),
        conv_b=column(i["a_conv_b_2"]), ga_b=column(i["a_gate_a_b_2"]), gx_b=column(i["a_gate_x_b_2"]),
        lam=column(i["a_lambda_2"]), a_ffn=column(i["a_ffn_norm_2"]), kv_norm=column(i["kv_norm_2"]),
        b_norm=column(i["b_norm_2"]), b_ffn=column(i["b_ffn_norm_2"]),
        diff_lam=np.broadcast_to(i["diff_lam"].reshape(1, 256), (P, 256)))
    x = np.concatenate([i["x"][0], i["ctx"][0]], 0)
    spread = lambda v: np.ascontiguousarray(np.broadcast_to(v, (P,) + v.shape))
    arrays = dict(
        xT=np.ascontiguousarray(x.T.reshape(DC, P, 2 * T).transpose(1, 0, 2)),
        w=np.concatenate(w, 0), ada_w=np.ascontiguousarray(ada).reshape(N_MODS * DC, P, D),
        vec=np.ascontiguousarray(np.concatenate([vecs[name] for name in VEC], 1)),
        positions=np.ascontiguousarray(i["positions_2"][0].reshape(TT, P).T),
        subln_g=spread(i["diff_subln_g"][0]), k_norm=spread(i["k_norm_2"]), q_norm=spread(i["b_q_norm_2"][0]))
    arrays.update(constants())
    return arrays


def kernel(**inputs):
    import concourse.bacc as bacc
    from concourse.bass_utils import run_bass_kernel_spmd

    nc = bacc.Bacc("TRN2", target_bir_lowering=False, num_devices=1)
    arrays = lay_out({name: np.asarray(v) for name, v in inputs.items()})
    maps, aps = {}, {}
    for name, v in arrays.items():
        maps[f"in_{name}"] = v
        aps[name] = nc.dram_tensor(f"in_{name}", v.shape, mybir.dt.from_np(v.dtype), kind="ExternalInput").ap()
    out = nc.dram_tensor("out_x", (P, DC, T), F32, kind="ExternalOutput").ap()
    build(nc, aps, out)
    got = run_bass_kernel_spmd(nc, [maps], core_ids=[0]).results[0]["out_x"]
    return np.ascontiguousarray(got.transpose(2, 1, 0).reshape(1, T, D))
```

```python
import math
from contextlib import ExitStack

import numpy as np

import concourse.bass as bass
from concourse import mybir

ALU = mybir.AluOpType
ACT = mybir.ActivationFunctionType
AX = mybir.AxisListType
F32 = mybir.dt.float32
F32R = mybir.dt.float32r
I32 = mybir.dt.int32

P = 128
D = 1024
DC = D // P
T = 256
TT = T // P
F = 2816
FC = F // P
W_OUT_PARTS = (8, 7, 7)
EPS = 1e-6
RING = 4
AHEAD = RING - 1
HEADS = 8
LAM_INIT = 0.8 - 0.6 * math.exp(-0.3)
DIFF_SCALE = 64 ** -0.5
DIL_SCALE = 128 ** -0.5
NEG = -1e30
N_MODS = 18
MODS_FIRST = 2

STAGES = [
    dict(kind="ffn", mod=0, n=2 * T, ada=(2, 13)),
    dict(kind="pool", mod=3, n=2 * T),
    dict(kind="ffn", mod=6, n=2 * T, ada=(13, 18)),
    dict(kind="ffn", mod=9, n=2 * T, ada=None),
    dict(kind="diff", mod=12, n=2 * T),
    dict(kind="ffn", mod=15, n=T, ada=None),
    dict(kind="final", n=T),
    dict(kind="lru", n=T),
    dict(kind="ffn", gain="a_ffn", mod=None, n=T, ada=None),
    dict(kind="dil", n=T),
    dict(kind="ffn", gain="b_ffn", mod=None, n=T, ada=None),
]
UNITS = dict(ffn=2 * FC + DC * 3, pool=2, diff=24 + 8, final=0, lru=16 + 2 + 8, dil=12 + 24 + 8)
CHUNKS = dict(ffn=2 * FC + DC, pool=DC, diff=DC, final=0, lru=16 + DC, dil=DC)
GROUPS = dict(diff=6, dil=9)
H_PARTS = (range(0, 3), range(3, 6), range(6, DC))
T_SETS = dict(ffn=1, pool=1, diff=1, lru=1, dil=2)
H_SETS = dict(ffn=1, pool=1, diff=1, lru=1, dil=2)


def plan():
    u = c = norms = ts = hs = p = f = q = 0
    for s in STAGES:
        s.update(q0=q * DC, u0=u, c0=c, norm_i=norms, t0=ts * DC, h0=hs * DC, p0=p, f0=f)
        u += UNITS[s["kind"]]
        c += CHUNKS[s["kind"]]
        norms += 1
        ts += T_SETS.get(s["kind"], 0)
        hs += H_SETS.get(s["kind"], 0)
        q += s["kind"] != "ffn"
        p += GROUPS.get(s["kind"], 0)
        f += FC if s["kind"] == "ffn" else 0
    return u


VEC = {}


def vec_columns():
    at = 0
    for name, n in (("c", 16), ("ada_b", 144), ("norm_g", 48), ("pool_scale", 8), ("final_g", 8),
                    ("a_norm", 8), ("conv_w", 32), ("conv_b", 8), ("ga_b", 8), ("gx_b", 8), ("lam", 8),
                    ("a_ffn", 8), ("kv_norm", 8), ("b_norm", 8), ("b_ffn", 8), ("diff_lam", 256)):
        VEC[name] = (at, n)
        at += n
    return at


NV = vec_columns()


class Tally:

    def __init__(self, eng, sem):
        self.eng, self.sem, self.n, self.marks = eng, sem, 0, 0

    def mark(self, ins):
        ins.then_inc(self.sem, 1)
        self.n = self.n + 1
        self.marks += 1

    def sync(self):
        self.eng.wait_ge(self.sem, self.n)

    def loop(self, first, end, per, body):
        base = self.n
        if end - first == 1:
            body(first)
        else:
            with self.eng.Fori(first, end) as i:
                self.n = base + (i - first) * per
                before = self.marks
                body(i)
                assert self.marks - before == per, (self.marks - before, per)
        self.n = base + (end - first) * per


def loop(eng, first, end, body):
    if end - first == 1:
        body(first)
    elif end > first:
        with eng.Fori(first, end) as i:
            body(i)


def build(nc, a, out, stages=None):
    TOTAL = plan()
    stages = STAGES if stages is None else STAGES[:stages]
    TOTAL = stages[-1]["u0"] + UNITS[stages[-1]["kind"]]

    with ExitStack() as ctx:
        def sb(name, shape, dt=F32, c=ctx):
            return c.enter_context(nc.sbuf_tensor(name, shape, dt))

        def sem(name):
            return ctx.enter_context(nc.semaphore(name))

        X = sb("X", [P, DC, 2 * T])
        H_hi = sb("H_hi", [P, DC, 2 * T], F32R)
        H_lo = sb("H_lo", [P, DC, 2 * T], F32R)
        raw = sb("raw", [P, RING, D])
        W_hi = sb("W_hi", [P, RING, D], F32R)
        W_lo = sb("W_lo", [P, RING, D], F32R)
        ada_w = sb("ada_w", [P, 2, D])
        vec = sb("vec", [P, NV])
        ident = sb("ident", [P, P])
        ones = sb("ones", [P, P])
        silu_c = sb("silu_c", [P, DC, 32])
        mods = sb("mods", [P, N_MODS, DC, 2])
        ada_T = sb("ada_T", [P, DC, 32])
        gain = sb("gain", [P, DC, 2])
        gate = sb("gate", [P, DC, 2])
        ssq = sb("ssq", [P, 2 * T])
        work = sb("work", [P, 3, 2 * T])
        std = sb("std", [P, 4])
        rstd = sb("rstd", [P, 4])
        sp8 = sb("sp8", [P, DC])
        lam = sb("lam", [P, 4])
        b_cos = sb("b_cos", [P, TT, 32])
        b_sin = sb("b_sin", [P, TT, 32])
        stat = sb("stat", [P, 64])
        with ExitStack() as c:
            G_hi = sb("G_hi", [P, FC, 2 * T], F32R, c)
            G_lo = sb("G_lo", [P, FC, 2 * T], F32R, c)
        with ExitStack() as c:
            sp_t = sb("sp_t", [P, 4, DC], F32, c)
            pos = sb("pos", [P, TT], I32, c)
            posf = sb("posf", [P, TT], F32, c)
            inv_freq = sb("inv_freq", [P, 16], F32, c)
            trig = sb("trig", [P, 5, TT, 16], F32, c)
            dots = sb("dots", [P, 2, 64], F32, c)
            ada_first = sb("ada_first", [P, MODS_FIRST * 8, D], F32, c)
        with ExitStack() as c:
            z_hi = sb("z_hi", [P, 4, D], F32R, c)
            z_lo = sb("z_lo", [P, 4, D], F32R, c)
            mix = sb("mix", [P, 4, TT, T], F32, c)
            mix_hi = sb("mix_hi", [P, 4, TT, T], F32R, c)
            mix_lo = sb("mix_lo", [P, 4, TT, T], F32R, c)
        with ExitStack() as c:
            d_KN = sb("d_KN", [P, 4, D], F32, c)
            d_QN = sb("d_QN", [P, TT, D], F32, c)
            d_VN = sb("d_VN", [P, 4, D], F32, c)
            d_KT = sb("d_KT", [P, HEADS, 2 * T], F32, c)
            d_QT = sb("d_QT", [P, HEADS, T], F32, c)
            d_P = sb("d_P", [P, 2, 2, 2 * T], F32, c)
            d_A = sb("d_A", [P, 2, 2 * T], F32, c)
            d_AT = sb("d_AT", [P, 2, 4, P], F32, c)
            d_cos = sb("d_cos", [P, TT, 64], F32, c)
            d_sin = sb("d_sin", [P, TT, 64], F32, c)
            d_g = sb("d_g", [P, P], F32, c)
        d_ON = d_KN[:, 0:TT, :]
        with ExitStack() as c:
            l_G = sb("l_G", [P, DC, T], F32, c)
            l_XB = sb("l_XB", [P, DC, T + 3], F32, c)
            l_XC = sb("l_XC", [P, DC, T], F32, c)
            l_R = sb("l_R", [P, DC, T], F32, c)
            l_I = sb("l_I", [P, DC, T], F32, c)
            l_A = sb("l_A", [P, DC, T], F32, c)
            l_T = sb("l_T", [P, DC, T], F32, c)
            l_H = sb("l_H", [P, DC, T], F32, c)
        with ExitStack() as c:
            b_N = sb("b_N", [P, 2, TT, 512], F32, c)
            b_VN = sb("b_VN", [P, TT, 3, T], F32, c)
            b_KT = sb("b_KT", [P, 6, T], F32, c)
            b_QT = sb("b_QT", [P, 24, T], F32, c)
            b_S = sb("b_S", [P, 3, 768], F32, c)
            b_PT = sb("b_PT", [P, 2, 768], F32, c)
            b_mask = sb("b_mask", [P, TT, 768], F32, c)
            b_gk = sb("b_gk", [P, 3, P], F32, c)
            b_gq = sb("b_gq", [P, 3, P], F32, c)
            b_ra = sb("b_ra", [P, TT, 4, 32], F32, c)
            b_rb = sb("b_rb", [P, TT, 4, 32], F32, c)

        PS = ctx.enter_context(nc.psum_tensor("PS", [P, 8, 512], F32))
        PSf = PS[:, :, :].rearrange("p b n -> p (b n)")
        ADA_BANK, SUM_BANK, BC_BANK = 4, 6, 7

        raw_ld = [sem(f"raw_ld{i}") for i in range(RING)]
        hi_ready = sem("hi_ready")
        lo_ready = sem("lo_ready")
        unit_done = sem("unit_done")
        psum_free = sem("psum_free")
        proj_taken = sem("proj_taken")
        in_vec, in_x, in_c, in_pos = sem("in_vec"), sem("in_x"), sem("in_c"), sem("in_pos")
        ada_ld = [sem(f"ada_ld{i}") for i in range(2)]
        first_ld = [sem(f"first_ld{i}") for i in range(4)]
        stage_ld = sem("stage_ld")
        region_free = sem("region_free")
        stored = sem("stored")
        start_ready = sem("start_ready")
        start_act = sem("start_act")
        silu_c_ready = sem("silu_c_ready")
        ada_used = sem("ada_used")
        first_used = sem("first_used")
        ada_taken = sem("ada_taken")
        vself = sem("vself")
        ssq_ready = sem("ssq_ready")
        xs_ready = sem("xs_ready")
        xsq_ready = sem("xsq_ready")
        norm_pe = sem("norm_pe")
        norm_sd = sem("norm_sd")
        norm_rs = sem("norm_rs")
        t_ready = sem("t_ready")
        h_hi_ready = sem("h_hi_ready")
        h_ready = sem("h_ready")
        silu_ready = sem("silu_ready")
        gu_ready = sem("gu_ready")
        z_done = sem("z_done")
        z_hi_ready, z_ready = sem("z_hi_ready"), sem("z_ready")
        mix_hi_ready, mix_ready = sem("mix_hi_ready"), sem("mix_ready")
        mix_done = sem("mix_done")
        kn_ready = sem("kn_ready")
        tp_done = sem("tp_done")
        tp_taken = sem("tp_taken")
        s_done = sem("s_done")
        nb_ready = sem("nb_ready")
        p_ready = sem("p_ready")
        a_ready = sem("a_ready")
        o_done = sem("o_done")
        o_hi = sem("o_hi")
        o_taken = sem("o_taken")
        o_sd = sem("o_sd")
        on_ready = sem("on_ready")
        ot_done = sem("ot_done")
        oh_hi, oh_ready = sem("oh_hi"), sem("oh_ready")
        sq_done = sem("sq_done")
        ss_ready = sem("ss_ready")
        sd_done = sem("sd_done")
        gelu_done = sem("gelu_done")
        xc_ready = sem("xc_ready")
        xc_hi, xc_lo = sem("xc_hi"), sem("xc_lo")
        sig_done = sem("sig_done")
        yr_ready = sem("yr_ready")
        a_t_done = sem("a_t_done")
        om_ready = sem("om_ready")
        sqrt_done = sem("sqrt_done")
        y_ready = sem("y_ready")
        y_hi, y_lo = sem("y_hi"), sem("y_lo")

        def V(name):
            at, n = VEC[name]
            return vec[:, at:at + n]

        def halves(n):
            return [(0, slice(0, T))] + ([(1, slice(T, 2 * T))] if n > T else [])

        block = ctx.enter_context(nc.Block())

        @block.sync
        def _(sp):
            sp.dma_start(vec[:, :], a["vec"]).then_inc(in_vec, 16)
            sp.dma_start(ident[:, :], a["ident"]).then_inc(in_c, 16)
            sp.dma_start(pos[:, :], a["positions"]).then_inc(in_pos, 16)
            sp.dma_start(inv_freq[:, :], a["inv_freq"]).then_inc(in_pos, 16)
            sp.dma_start(X[:, :, :], a["xT"]).then_inc(in_x, 16)

            def load(u, slot, blocks=8):
                sp.wait_ge(lo_ready, u + 1)
                sp.dma_start(raw[:, slot, 0:blocks * P], a["w"][u, :, 0:blocks * P]).then_inc(raw_ld[slot], 16)

            def units(u0, n):
                def body(i):
                    for k in range(4):
                        load(u0 + 4 * i + k, (u0 + k) % RING)
                loop(sp, 0, n // 4, body)
                for k in range(n - n % 4, n):
                    load(u0 + k, (u0 + k) % RING)

            n4 = MODS_FIRST * 8 // 4
            for q in range(4):
                if q == 3:
                    for u in range(AHEAD):
                        load(u, u)
                sp.dma_start(ada_first[:, n4 * q:n4 * q + n4, :],
                             a["ada_w"][n4 * q:n4 * q + n4].rearrange("m p d -> p m d")).then_inc(first_ld[q], 16)

            for s in stages:
                if s["kind"] == "ffn":
                    skip = AHEAD if s is stages[0] else 0
                    units(s["u0"] + skip, 2 * FC - skip)
                    u1 = s["u0"] + 2 * FC

                    def body(i):
                        for k in range(4):
                            for part, blocks in enumerate(W_OUT_PARTS):
                                load(u1 + 12 * i + 3 * k + part, (u1 + 3 * k + part) % RING, blocks)
                    loop(sp, 0, 2, body)
                else:
                    units(s["u0"], UNITS[s["kind"]])
            last = stages[-1]
            for d in range(DC):
                sp.wait_ge(psum_free, RING + last["c0"] + CHUNKS[last["kind"]] - DC + d + 1)
                sp.dma_start(out[:, d, :], X[:, d, 0:out.shape[2]]).then_inc(stored, 16)
            sp.wait_ge(stored, 16 * DC)

        @block.gpsimd
        def _(pool):
            def mod_weights(m):
                for part in range(8):
                    pool.wait_ge(ada_used, (m - MODS_FIRST) * 8 + (part + 1))
                    pool.dma_start(ada_w[:, part % 2, :], a["ada_w"][m * 8 + part]).then_inc(ada_ld[part % 2], 16)

            pool.wait_ge(first_used, 8)
            turn = 0
            for s in stages:
                if s.get("ada"):
                    loop(pool, s["ada"][0], s["ada"][1], mod_weights)
                consts = {
                    "pool": [(mix[:, :, :, :], "mix")],
                    "diff": [(d_cos[:, :, :], "d_cos"), (d_sin[:, :, :], "d_sin"), (d_g[:, :], "subln_g")],
                    "dil": [(b_mask[:, :, :], "mask"), (b_gk[:, :, :], "k_norm"), (b_gq[:, :, :], "q_norm")],
                }.get(s["kind"], [])
                if consts:
                    turn += 1
                    pool.wait_ge(region_free, turn)
                    for dst, name in consts:
                        pool.dma_start(dst, a[name]).then_inc(stage_ld, 16)

        @block.tensor
        def _(pe):
            pe.sem_inc(unit_done, RING)
            pe.sem_inc(ada_used, 2)

            def block3(out, slot, b, hi, lo, start, stop):
                w = slice(b * P, (b + 1) * P)
                pe.matmul(out, W_hi[:, slot, w], hi, start=start, stop=False)
                pe.matmul(out, W_hi[:, slot, w], lo, start=False, stop=False)
                return pe.matmul(out, W_lo[:, slot, w], hi, start=False, stop=stop)

            def ada_products(part, weights):
                for j in range(4):
                    mm = pe.matmul(PS[32 * j:32 * j + 32, ADA_BANK, 0:256], silu_c[:, part, :],
                                   weights[:, 256 * j:256 * j + 256], start=part == 0, stop=part == 7)
                return mm

            def ada_part(m, part):
                if part == 0:
                    pe.wait_ge(ada_taken, m)
                pe.wait_ge(ada_ld[part % 2], 16 * ((m - MODS_FIRST) * 4 + (part // 2 + 1)))
                ada_products(part, ada_w[:, part % 2, :]).then_inc(ada_used, 1)

            def norm(s, n):
                k = s["norm_i"]
                pe.wait_ge(ssq_ready, DC * (k + 1) - 1)
                for t in range(n // P):
                    pe.matmul(PS[:, SUM_BANK, t:t + 1], ssq[:, t * P:(t + 1) * P], ones[:, 0:1],
                              start=t == 0, stop=False)
                before = stages[k - 1] if k else None
                if before is None or before["kind"] == "ffn":
                    pe.wait_ge(ssq_ready, DC * (k + 1))
                    last_squares = work[:, 2, :]
                else:
                    pe.wait_ge(xsq_ready, before["q0"] + DC)
                    last_squares = work[:, (DC - 1) % 2, :]
                for t in range(n // P):
                    mm = pe.matmul(PS[:, SUM_BANK, t:t + 1], last_squares[:, t * P:(t + 1) * P], ones[:, 0:1],
                                   start=False, stop=t == n // P - 1)
                mm.then_inc(norm_pe, 1)
                pe.wait_ge(norm_rs, k + 1)
                for t in range(n // P):
                    mm = pe.matmul(PS[:, BC_BANK, t * P:(t + 1) * P], rstd[:, t:t + 1].to_broadcast([P, P]),
                                   ident[:, :], start=True, stop=True)
                mm.then_inc(norm_pe, 1)

            def linear(u0, c0, n_units, lo, hi, h_sem, h_base, h_per, ada=None):
                def unit(u, c, k):
                    pe.wait_ge(psum_free, c + 1)
                    pe.wait_ge(lo_ready, RING + (u + 1))
                    for kc in range(DC):
                        mm = block3(PS[:, (c0 + k) % RING, 0:hi - lo], (u0 + k) % RING, kc,
                                    H_hi[:, kc, lo:hi], H_lo[:, kc, lo:hi], kc == 0, kc == DC - 1)
                    mm.then_inc(unit_done, 1)

                for k in range(3):
                    pe.wait_ge(psum_free, c0 + k + 1)
                    pe.wait_ge(lo_ready, RING + u0 + k + 1)
                for kc in range(DC):
                    pe.wait_ge(h_sem, h_base + h_per * (kc + 1))
                    for k in range(3):
                        mm = block3(PS[:, (c0 + k) % RING, 0:hi - lo], (u0 + k) % RING, kc,
                                    H_hi[:, kc, lo:hi], H_lo[:, kc, lo:hi], kc == 0, kc == DC - 1)
                        if kc == DC - 1:
                            mm.then_inc(unit_done, 1)
                    if ada:
                        ada_part(ada[0], kc)
                unit(u0 + 3, c0 + 3, 3)

                def body(i, with_ada=False):
                    for k in range(4):
                        unit(u0 + 4 * i + k, c0 + 4 * i + k, k)
                        if with_ada:
                            ada_part(ada[0] + i, 2 * k)
                            ada_part(ada[0] + i, 2 * k + 1)
                n_ada = ada[1] - ada[0] if ada else 0
                if n_ada > 1:
                    loop(pe, 1, n_ada, lambda i: body(i, True))
                loop(pe, max(n_ada, 1), n_units // 4, body)

            def w_out(s, n):
                u1, c1 = s["u0"] + 2 * FC, s["c0"] + 2 * FC
                pe.wait_ge(gu_ready, 1 + s["f0"] + W_OUT_PARTS[0] + W_OUT_PARTS[1])

                def body(i):
                    for k in range(4):
                        pe.wait_ge(psum_free, c1 + 4 * i + (k + 1))
                        f = 0
                        for part, blocks in enumerate(W_OUT_PARTS):
                            pe.wait_ge(lo_ready, RING + u1 + 12 * i + (3 * k + part + 1))
                            if part == 2:
                                pe.wait_ge(gu_ready, 1 + s["f0"] + FC)
                            for b in range(blocks):
                                mm = block3(PS[:, (c1 + k) % RING, 0:n], (u1 + 3 * k + part) % RING, b,
                                            G_hi[:, f, 0:n], G_lo[:, f, 0:n], f == 0, f == FC - 1)
                                f += 1
                            mm.then_inc(unit_done, 1)
                loop(pe, 0, 2, body)

            def project(s, g, tiles, first_bank, col, h_first=None):
                p = s["p0"] + g
                pe.wait_ge(proj_taken, p + 1)
                for q in range(4):
                    if h_first is not None:
                        pe.wait_ge(h_ready, h_first + 2 * (q + 1))
                    u = s["u0"] + 4 * g + q
                    pe.wait_ge(lo_ready, RING + u + 1)
                    for t in range(tiles):
                        for k2 in range(2):
                            kc = 2 * q + k2
                            rows = slice(col + t * P, col + (t + 1) * P)
                            w = slice(k2 * 512, (k2 + 1) * 512)
                            o = PS[:, first_bank + t, :]
                            pe.matmul(o, H_hi[:, kc, rows], W_hi[:, u % RING, w], start=kc == 0, stop=False)
                            pe.matmul(o, H_hi[:, kc, rows], W_lo[:, u % RING, w], start=False, stop=False)
                            mm = pe.matmul(o, H_lo[:, kc, rows], W_hi[:, u % RING, w], start=False, stop=kc == 7)
                    mm.then_inc(unit_done, 1)

            n4 = MODS_FIRST * 8 // 4
            pe.wait_ge(silu_c_ready, 1)
            pe.wait_ge(in_c, 16)
            norm(stages[0], 2 * T)
            for m in range(MODS_FIRST):
                if m:
                    pe.wait_ge(ada_taken, m)
                for part in range(8):
                    if (8 * m + part) % n4 == 0:
                        pe.wait_ge(first_ld[(8 * m + part) // n4], 16)
                    ada_products(part, ada_first[:, 8 * m + part, :]).then_inc(first_used, 1)

            tp = 0
            its = 0
            for s in stages:
                n = s["n"]
                if s["kind"] == "ffn":
                    if s is not stages[0]:
                        norm(s, n)
                    linear(s["u0"], s["c0"], 2 * FC, 0, n, h_ready, s["h0"], 1, s["ada"])
                    w_out(s, n)

                elif s["kind"] == "pool":
                    norm(s, n)
                    pe.wait_ge(psum_free, RING + s["c0"])
                    for half in range(2):
                        u = s["u0"] + half
                        pe.wait_ge(lo_ready, RING + u + 1)
                        for t in range(4):
                            rows = slice(t * P, (t + 1) * P)
                            for g2 in range(2):
                                for k2 in range(2):
                                    kc = 4 * half + 2 * g2 + k2
                                    if t == 0 or half:
                                        pe.wait_ge(h_ready, s["h0"] + (DC if half else kc + 1))
                                    o = PS[:, t + 4 * half, g2 * T:(g2 + 1) * T]
                                    w = slice((2 * g2 + k2) * T, (2 * g2 + k2 + 1) * T)
                                    pe.matmul(o, H_hi[:, kc, rows], W_hi[:, u % RING, w], start=k2 == 0, stop=False)
                                    pe.matmul(o, H_hi[:, kc, rows], W_lo[:, u % RING, w], start=False, stop=False)
                                    mm = pe.matmul(o, H_lo[:, kc, rows], W_hi[:, u % RING, w], start=False, stop=k2 == 1)
                            mm.then_inc(z_done, 1)
                        pe.sem_inc(unit_done, 1)
                    pe.wait_ge(mix_ready, 4)
                    for c in range(DC):
                        pe.wait_ge(z_ready, 4 * (c // 4) + 4)
                        pe.wait_ge(psum_free, s["c0"] + c + 1)
                        w = slice(c * P, (c + 1) * P)
                        for q in range(2):
                            o = PS[:, (s["c0"] + c) % RING, q * T:(q + 1) * T]
                            for k in range(TT):
                                m_hi, m_lo = mix_hi[:, c // 2, k, :], mix_lo[:, c // 2, k, :]
                                pe.matmul(o, z_hi[:, TT * q + k, w], m_hi, start=k == 0, stop=False)
                                pe.matmul(o, z_hi[:, TT * q + k, w], m_lo, start=False, stop=False)
                                mm = pe.matmul(o, z_lo[:, TT * q + k, w], m_hi, start=False, stop=k == TT - 1)
                        mm.then_inc(mix_done, 1)

                elif s["kind"] == "diff":
                    norm(s, n)
                    for g in range(6):
                        project(s, g, 4 if g < 4 else TT, 4 * (g % 2), 0, s["h0"] if g == 0 else None)
                    for h in range(HEADS):
                        if h == 0:
                            pe.wait_ge(kn_ready, 6)
                            pe.wait_ge(proj_taken, s["p0"] + 6 + 2)
                            pe.wait_ge(in_c, 16)
                        pe.wait_ge(tp_taken, tp + 1)
                        for t in range(4):
                            mm = pe.transpose(PS[:, 4 + tp % 2, t * P:(t + 1) * P],
                                              d_KN[:, t, h * P:(h + 1) * P], ident[:, :])
                        mm.then_inc(tp_done, 1)
                        tp += 1
                    for hh in range(HEADS // 2):
                        pe.wait_ge(tp_taken, tp + 1)
                        for h2 in range(2):
                            for t in range(TT):
                                mm = pe.transpose(PS[:, 4 + tp % 2, (2 * h2 + t) * P:(2 * h2 + t + 1) * P],
                                                  d_QN[:, t, (2 * hh + h2) * P:(2 * hh + h2 + 1) * P], ident[:, :])
                        mm.then_inc(tp_done, 1)
                        tp += 1
                    pe.wait_ge(tp_taken, tp + 2)

                    def scores(it):
                        h, qt = divmod(it, TT)
                        if it >= 2:
                            pe.wait_ge(p_ready, its + it - 1)
                        for j in range(2):
                            rows = slice(64 * j, 64 * j + 64)
                            mm = pe.matmul(PS[:, 2 * (it % 2) + j, :], d_QT[rows, h, qt * P:(qt + 1) * P],
                                           d_KT[rows, h, :], start=True, stop=True)
                        mm.then_inc(s_done, 1)

                    def turn_p(it):
                        nonlocal tp
                        pe.wait_ge(a_ready, its + it + 1)
                        pe.wait_ge(tp_taken, tp + 1)
                        for k in range(4):
                            mm = pe.transpose(PS[:, 4 + tp % 2, k * P:(k + 1) * P],
                                              d_A[:, it % 2, k * P:(k + 1) * P], ident[:, :])
                        mm.then_inc(tp_done, 1)
                        tp += 1

                    def values(it, tp_of):
                        h, qt = divmod(it, TT)
                        pe.wait_ge(tp_taken, tp_of + 3)
                        if it >= 2:
                            pe.wait_ge(o_taken, its + it - 1)
                        for k in range(4):
                            mm = pe.matmul(PS[:, 6 + it % 2, 0:P], d_AT[:, it % 2, k, :],
                                           d_VN[:, k, h * P:(h + 1) * P], start=k == 0, stop=k == 3)
                        mm.then_inc(o_done, 1)

                    tp_first = tp
                    scores(0)
                    scores(1)
                    for it in range(2 * HEADS):
                        if it + 2 < 2 * HEADS:
                            scores(it + 2)
                        turn_p(it)
                        if it >= 1:
                            values(it - 1, tp_first + it - 1)
                    values(2 * HEADS - 1, tp_first + 2 * HEADS - 1)
                    its += 2 * HEADS
                    pe.wait_ge(o_taken, its)
                    pe.wait_ge(tp_taken, tp + 2)
                    for hh in range(HEADS // 2):
                        pe.wait_ge(on_ready, hh + 1)
                        for h2 in range(2):
                            for t in range(TT):
                                mm = pe.transpose(PS[:, 4 + hh, (2 * h2 + t) * P:(2 * h2 + t + 1) * P],
                                                  d_ON[:, t, (2 * hh + h2) * P:(2 * hh + h2 + 1) * P], ident[:, :])
                        mm.then_inc(ot_done, 1)
                    linear(s["u0"] + 24, s["c0"], 8, 0, T, oh_ready, 0, 1)

                elif s["kind"] == "final":
                    norm(s, n)

                elif s["kind"] == "lru":
                    norm(s, n)
                    linear(s["u0"], s["c0"], 16, 0, T, h_ready, s["h0"], 1)
                    for half in range(2):
                        u = s["u0"] + 16 + half
                        if half:
                            pe.wait_ge(psum_free, s["c0"] + 16 + RING)
                        pe.wait_ge(lo_ready, RING + u + 1)
                        for c in range(DC):
                            pe.wait_ge(xc_lo, c + 1)
                            mm = block3(PS[:, 4 - 4 * half + c // 2, (c % 2) * T:(c % 2 + 1) * T], u % RING, c,
                                        H_hi[:, c, T:2 * T], H_lo[:, c, T:2 * T], True, True)
                        mm.then_inc(unit_done, 1)
                    linear(s["u0"] + 18, s["c0"] + 16, 8, 0, T, y_lo, 0, 1)

                elif s["kind"] == "dil":
                    norm(s, n)

                    def turn_group(g):
                        nonlocal tp
                        pe.wait_ge(kn_ready, 6 + g + 1)
                        blocks = [(h, t) for h in range(2 if g < 3 else 4) for t in range(TT)]
                        for b0 in range(0, len(blocks), 4):
                            pe.wait_ge(tp_taken, tp + 1)
                            for b, (h, t) in enumerate(blocks[b0:b0 + 4]):
                                mm = pe.transpose(PS[:, 4 + tp % 2, b * P:(b + 1) * P],
                                                  b_N[:, g % 2, t, h * P:(h + 1) * P], ident[:, :])
                            mm.then_inc(tp_done, 1)
                            tp += 1

                    for g in range(9):
                        project(s, g, TT, 2 * (g % 2), 0 if g < 3 else T,
                                {0: s["h0"], 3: s["h0"] + DC}.get(g))
                        if g:
                            turn_group(g - 1)
                    def scores(it):
                        h, qt = divmod(it, TT)
                        w = (qt + 1) * P
                        if it >= 2:
                            pe.wait_ge(nb_ready, its + it - 1)
                        for g in range(3):
                            at = (it % 2) * 1024 + g * w
                            mm = pe.matmul(PSf[:, at:at + w], b_QT[:, g * HEADS + h, qt * P:(qt + 1) * P],
                                           b_KT[:, 2 * g + h // 4, 0:w], start=True, stop=True)
                        mm.then_inc(s_done, 1)

                    def turn_p(it):
                        qt = it % TT
                        pe.wait_ge(a_ready, its + it + 1)
                        if it >= 2:
                            pe.wait_ge(o_taken, its + it - 1)
                        for b in range(3 * (qt + 1)):
                            at = 2048 + (it % 2) * 1024 + b * P
                            mm = pe.transpose(PSf[:, at:at + P], b_S[:, it % 3, b * P:(b + 1) * P], ident[:, :])
                        mm.then_inc(tp_done, 1)

                    def values(it):
                        h, qt = divmod(it, TT)
                        pe.wait_ge(tp_taken, tp + it + 3)
                        at = 2048 + (it % 2) * 1024 + 896
                        for g in range(3):
                            for k in range(qt + 1):
                                b = g * (qt + 1) + k
                                mm = pe.matmul(PSf[:, at:at + P], b_VN[:, k, g, (h // 4) * P:(h // 4 + 1) * P],
                                               b_PT[:, it % 2, b * P:(b + 1) * P],
                                               start=b == 0, stop=b == 3 * (qt + 1) - 1)
                        mm.then_inc(o_done, 1)

                    pe.wait_ge(proj_taken, s["p0"] + 9 + 2)
                    pe.wait_ge(tp_taken, tp + 2)
                    scores(0)
                    scores(1)
                    turn_group(8)
                    pe.wait_ge(tp_taken, tp + 2)
                    for it in range(2 * HEADS):
                        if it + 2 < 2 * HEADS:
                            scores(it + 2)
                        turn_p(it)
                        if it >= 1:
                            values(it - 1)
                    values(2 * HEADS - 1)
                    tp += 2 * HEADS
                    its += 2 * HEADS
                    pe.wait_ge(o_taken, its)
                    linear(s["u0"] + 36, s["c0"], 8, 0, T, o_taken, its - DC, 1)

        @block.scalar
        def _(act):
            act.sem_inc(tp_taken, 2)

            def split(base, i, stride, k):
                if isinstance(i, int) and base + stride * i + k >= TOTAL:
                    return
                slot = (base + k) % RING
                act.wait_ge(raw_ld[slot], 16 * (stride // RING) * i + 16 * ((base + k) // RING + 1))
                act.wait_ge(unit_done, stride * i + (base + k + 1))
                act.copy(W_hi[:, slot, :], raw[:, slot, :]).then_inc(hi_ready, 1)

            def split_units(s, first, n):
                def body(i):
                    for k in range(4):
                        split(s["u0"] + AHEAD + first, i, 4, k)
                loop(act, 0, n // 4, body)

            def norm(s, n):
                act.wait_ge(norm_pe, 2 * s["norm_i"] + 1)
                act.activation(std[:, 0:n // P], PS[:, SUM_BANK, 0:n // P], ACT.Sqrt, bias=EPS, scale=1.0 / D)\
                   .then_inc(norm_sd, 1)

            def square(s, n, d, base_d):
                act.wait_ge(ssq_ready, DC * (s["norm_i"] + 1) + base_d + (d - 1))
                act.activation(work[:, d % 2, 0:n], X[:, bass.ds(base_d + d, 1), 0:n] if not isinstance(base_d, int)
                               else X[:, base_d + d, 0:n], ACT.Square).then_inc(xsq_ready, 1)

            def linear_out(s, u_off, c_off, n):
                def body(i):
                    for k in range(4):
                        split(s["u0"] + AHEAD + u_off, i, 4, k)
                        act.wait_ge(psum_free, s["c0"] + c_off + 4 * i + (k + RING + 1))
                        square(s, n, k, 4 * i)
                loop(act, 0, 2, body)

            def high_parts(s, n, t0, shift, dst, ds=range(DC)):
                for d in ds:
                    act.wait_ge(t_ready, t0 + d + 1)
                    for h, cols in halves(n):
                        if shift is None:
                            ins = act.copy(dst(d, cols), work[:, d % 2, cols])
                        else:
                            ins = act.activation(dst(d, cols), work[:, d % 2, cols], ACT.Identity,
                                                 bias=mods[:, shift, d, h:h + 1])
                    ins.then_inc(h_hi_ready, 1)

            act.wait_ge(in_vec, 16)
            act.wait_ge(start_ready, 1)
            act.activation(silu_c[:, :, 0:2], V("c").rearrange("p (d s) -> p d s", s=2), ACT.Silu)\
               .then_inc(silu_c_ready, 1)
            act.wait_ge(start_ready, 2)
            act.activation(sp_t[:, 1, :], sp_t[:, 0, :], ACT.Exp, scale=-1.0)
            act.activation(lam[:, 2:4], lam[:, 0:2], ACT.Exp).then_inc(start_act, 1)
            act.wait_ge(start_ready, 3)
            act.activation(trig[:, 3:5, :, :], trig[:, 1:3, :, :], ACT.Sin).then_inc(start_act, 1)
            norm(stages[0], 2 * T)
            for k in range(AHEAD):
                split(0, 0, 4, k)

            tp = its = 0
            for s in stages:
                n = s["n"]
                if s is not stages[0]:
                    norm(s, n)
                if s["kind"] == "ffn":
                    high_parts(s, n, s["t0"], s["mod"], lambda d, cols: H_hi[:, d, cols])

                    def body(i):
                        for k in range(4):
                            split(s["u0"] + AHEAD, i, 4, k)
                            if k % 2 == 0:
                                act.wait_ge(unit_done, RING + s["u0"] + 4 * i + (k + 1))
                                act.wait_ge(psum_free, s["c0"] + 4 * i + (k + 2))
                                act.activation(work[:, k // 2, 0:n], PS[:, (s["c0"] + k) % RING, 0:n], ACT.Silu)\
                                   .then_inc(silu_ready, 1)
                    loop(act, 0, FC // 2, body)

                    def body(i):
                        for k in range(12):
                            split(s["u0"] + 2 * FC + AHEAD, i, 12, k)
                    if s is stages[-1]:
                        body(0)
                        body(1)
                    else:
                        loop(act, 0, 2, body)

                elif s["kind"] == "pool":
                    high_parts(s, n, s["t0"], s["mod"], lambda d, cols: H_hi[:, d, cols])
                    act.wait_ge(stage_ld, 16)
                    for g in range(4):
                        act.copy(mix_hi[:, g, :, :], mix[:, g, :, :]).then_inc(mix_hi_ready, 1)
                    for half in range(2):
                        for t in range(4):
                            act.wait_ge(z_done, 4 * half + t + 1)
                            act.copy(z_hi[:, t, half * 512:half * 512 + 512], PS[:, t + 4 * half, :])\
                               .then_inc(z_hi_ready, 1)
                    for k in range(2):
                        split(s["u0"] + AHEAD, 0, 4, k)
                    for d in range(DC):
                        act.wait_ge(psum_free, RING + s["c0"] + d + 1)
                        square(s, n, d, 0)

                elif s["kind"] == "diff":
                    high_parts(s, n, s["t0"], s["mod"], lambda d, cols: H_hi[:, d, cols])
                    split_units(s, 0, 24)
                    for h in range(HEADS):
                        act.wait_ge(tp_done, tp + 1)
                        act.copy(d_KT[:, h, :], PS[:, 4 + tp % 2, :]).then_inc(tp_taken, 1)
                        tp += 1
                    for hh in range(HEADS // 2):
                        act.wait_ge(tp_done, tp + 1)
                        act.copy(d_QT[:, 2 * hh:2 * hh + 2, :],
                                 PS[:, 4 + tp % 2, :].rearrange("p (h t) -> p h t", h=2)).then_inc(tp_taken, 1)
                        tp += 1

                    def exps(it):
                        act.wait_ge(nb_ready, its + it + 1)
                        if it >= 2:
                            act.wait_ge(a_ready, its + it - 1)
                        for j in range(2):
                            at = 2 * (it % 2) + j
                            ins = act.activation(d_P[:, it % 2, j, :], PS[:, at, :], ACT.Exp,
                                                 bias=stat[:, 4 + at:5 + at], scale=DIFF_SCALE,
                                                 accum_out=stat[:, 8 + at:9 + at])
                        ins.then_inc(p_ready, 1)

                    def copy_p(it):
                        nonlocal tp
                        act.wait_ge(tp_done, tp + 1)
                        if it >= 2:
                            act.wait_ge(o_done, its + it - 1)
                        act.copy(d_AT[:, it % 2, :, :], PS[:, 4 + tp % 2, :].rearrange("p (k q) -> p k q", k=4))\
                           .then_inc(tp_taken, 1)
                        tp += 1

                    def take_o(it):
                        h, qt = divmod(it, TT)
                        act.wait_ge(o_done, its + it + 1)
                        act.copy(d_ON[:, qt, h * P:(h + 1) * P], PS[:, 6 + it % 2, 0:P])
                        if it >= 2:
                            act.wait_ge(o_taken, its + it - 1)
                        act.activation(work[:, it % 2, 0:P], PS[:, 6 + it % 2, 0:P], ACT.Square,
                                       accum_out=stat[:, 16 + it:17 + it]).then_inc(o_taken, 1)

                    exps(0)
                    for it in range(2 * HEADS):
                        if it + 1 < 2 * HEADS:
                            exps(it + 1)
                        copy_p(it)
                        if it >= 1:
                            take_o(it - 1)
                    take_o(2 * HEADS - 1)
                    its += 2 * HEADS
                    act.wait_ge(o_taken, its)
                    act.activation(stat[:, 32:48], stat[:, 16:32], ACT.Sqrt, bias=EPS, scale=1.0 / P)\
                       .then_inc(o_sd, 1)
                    for hh in range(HEADS // 2):
                        act.wait_ge(ot_done, hh + 1)
                        act.copy(H_hi[:, 2 * hh:2 * hh + 2, 0:T],
                                 PS[:, 4 + hh, :].rearrange("p (h t) -> p h t", h=2)).then_inc(oh_hi, 1)
                    linear_out(s, 24, 0, T)

                elif s["kind"] == "final":
                    for d in range(DC):
                        act.wait_ge(xs_ready, d + 1)
                        square(s, T, d, 0)

                elif s["kind"] == "lru":
                    high_parts(s, n, s["t0"], None, lambda d, cols: H_hi[:, d, cols])
                    for k in range(16):
                        split(s["u0"] + AHEAD, 0, 4, k)
                        d = k // 2
                        if k % 2:
                            act.wait_ge(xc_ready, d + 1)
                            act.copy(H_hi[:, d, T:2 * T], l_XC[:, d, :]).then_inc(xc_hi, 1)
                            act.wait_ge(unit_done, RING + s["u0"] + k + 1)
                            act.activation(l_G[:, d, :], PS[:, (s["c0"] + k) % RING, 0:T], ACT.Gelu_apprx_tanh)\
                               .then_inc(gelu_done, 1)
                    for half, (dst, bias) in enumerate(((l_R, "ga_b"), (l_I, "gx_b"))):
                        split(s["u0"] + AHEAD, 0, 4, 16 + half)
                        act.wait_ge(unit_done, RING + s["u0"] + 16 + half + 1)
                        for c in range(DC):
                            act.activation(dst[:, c, :], PS[:, 4 - 4 * half + c // 2, (c % 2) * T:(c % 2 + 1) * T],
                                           ACT.Sigmoid, bias=V(bias)[:, c:c + 1]).then_inc(sig_done, 1)
                    for q in range(4):
                        two = slice(2 * q, 2 * q + 2)
                        act.wait_ge(yr_ready, q + 1)
                        act.activation(l_A[:, two, :], l_H[:, two, :], ACT.Exp, scale=-1.0)
                        act.activation(l_T[:, two, :], l_H[:, two, :], ACT.Tanh).then_inc(a_t_done, 1)
                    for q in range(4):
                        act.wait_ge(om_ready, q + 1)
                        act.activation(l_T[:, 2 * q:2 * q + 2, :], l_T[:, 2 * q:2 * q + 2, :], ACT.Sqrt)\
                           .then_inc(sqrt_done, 1)
                    for q in range(4):
                        act.wait_ge(y_ready, q + 1)
                        act.copy(H_hi[:, 2 * q:2 * q + 2, 0:T], l_H[:, 2 * q:2 * q + 2, :]).then_inc(y_hi, 1)
                    linear_out(s, 18, 16, T)

                elif s["kind"] == "dil":
                    high_parts(s, n, s["t0"], None, lambda d, cols: H_hi[:, d, cols])

                    def copy_group(g):
                        nonlocal tp
                        for b in range(1 if g < 3 else 2):
                            act.wait_ge(tp_done, tp + 1)
                            h = 4 * (g - 3) + 2 * b
                            dst = b_KT[:, 2 * g:2 * g + 2, :] if g < 3 else b_QT[:, h:h + 2, :]
                            act.copy(dst, PS[:, 4 + tp % 2, :].rearrange("p (h t) -> p h t", h=2)).then_inc(tp_taken, 1)
                            tp += 1

                    for g in range(9):
                        split_units(s, 4 * g, 4)
                        if g < 3:
                            high_parts(s, n, s["t0"] + DC, None, lambda d, cols: H_hi[:, d, T:2 * T], H_PARTS[g])
                            act.wait_ge(h_ready, s["h0"] + DC + H_PARTS[g].stop)
                        heads = 2 if g < 3 else 4
                        act.wait_ge(unit_done, RING + s["u0"] + 4 * g + 4)
                        if g:
                            act.wait_ge(ss_ready, g)
                        for t in range(TT):
                            ins = act.activation(work[:, t, 0:heads * P], PS[:, 2 * (g % 2) + t, 0:heads * P], ACT.Square)
                        ins.then_inc(sq_done, 1)
                        act.wait_ge(ss_ready, g + 1)
                        act.activation(stat[:, 8:8 + TT * heads], stat[:, 0:TT * heads], ACT.Sqrt, bias=EPS, scale=1.0 / P)\
                           .then_inc(sd_done, 1)
                        if g:
                            copy_group(g - 1)
                    copy_group(8)

                    def exps(it):
                        w = 3 * (it % TT + 1) * P
                        act.wait_ge(nb_ready, its + it + 1)
                        act.activation(b_S[:, it % 3, 0:w], b_S[:, it % 3, 0:w], ACT.Exp,
                                       bias=stat[:, 32 + it % 2:33 + it % 2],
                                       accum_out=stat[:, 34 + it % 2:35 + it % 2]).then_inc(p_ready, 1)

                    def copy_p(it):
                        w = 3 * (it % TT + 1) * P
                        at = 2048 + (it % 2) * 1024
                        act.wait_ge(tp_done, tp + it + 1)
                        if it >= 2:
                            act.wait_ge(o_done, its + it - 1)
                        act.copy(b_PT[:, it % 2, 0:w], PSf[:, at:at + w]).then_inc(tp_taken, 1)

                    def take_o(it):
                        h, qt = divmod(it, TT)
                        act.wait_ge(o_done, its + it + 1)
                        act.copy(H_hi[:, h, qt * P:(qt + 1) * P],
                                 PSf[:, (it % 2) * 1024 + 2944:(it % 2) * 1024 + 3072]).then_inc(o_hi, 1)

                    exps(0)
                    for it in range(2 * HEADS):
                        if it + 1 < 2 * HEADS:
                            exps(it + 1)
                        copy_p(it)
                        if it >= 1:
                            take_o(it - 1)
                    take_o(2 * HEADS - 1)
                    tp += 2 * HEADS
                    its += 2 * HEADS
                    linear_out(s, 36, 0, T)

        @block.vector
        def _(ve):
            own = Tally(ve, vself)
            ve.sem_inc(lo_ready, RING)
            ve.sem_inc(psum_free, RING)
            ve.sem_inc(proj_taken, 2)
            ve.sem_inc(gu_ready, 1)

            def step(ins):
                own.mark(ins)
                own.sync()

            def split(base, i, stride, k):
                if isinstance(i, int) and base + stride * i + k >= TOTAL:
                    return
                slot = (base + k) % RING
                ve.wait_ge(hi_ready, stride * i + (base + k + 1))
                ve.tensor_tensor(W_lo[:, slot, :], raw[:, slot, :], W_hi[:, slot, :], ALU.subtract).then_inc(lo_ready, 1)

            def split_units(s, first, n):
                def body(i):
                    for k in range(4):
                        split(s["u0"] + AHEAD + first, i, 4, k)
                own.loop(0, n // 4, 0, body)

            def take_mod(m):
                if isinstance(m, int) and m < MODS_FIRST:
                    ve.wait_ge(first_used, 8 * m + 8)
                else:
                    ve.wait_ge(ada_used, (m - MODS_FIRST) * 8 + 10)
                step(ve.transpose(ada_T[:, :, :], PS[:, ADA_BANK, 0:256].rearrange("p (b c) -> p b c", c=32)))
                ve.sem_inc(ada_taken, 1)
                for h in range(2):
                    ins = ve.tensor_tensor(mods[:, m, :, h], ada_T[:, :, h],
                                           V("ada_b")[:, bass.ds(m * DC, DC)], ALU.add)
                step(ins)

            def add_square(q, d, n):
                if not isinstance(q, int) or q:
                    ve.wait_ge(ssq_ready, q)
                squares = ve.tensor_tensor(work[:, 2, 0:n], X[:, d, 0:n], X[:, d, 0:n], ALU.mult)
                if d == DC - 1:
                    squares.then_inc(ssq_ready, 1)
                    return
                step(squares)
                ve.tensor_tensor(ssq[:, 0:n], ssq[:, 0:n], work[:, 2, 0:n], ALU.add).then_inc(ssq_ready, 1)

            def gains(s):
                if s.get("mod") is not None:
                    own.sync()
                    j = s["mod"] + 1
                    g = V("norm_g")[:, (s["mod"] // 3) * DC:(s["mod"] // 3 + 1) * DC]
                    for h in range(2):
                        ins = ve.scalar_tensor_tensor(gain[:, :, h], mods[:, j, :, h], 1.0, g, ALU.add, ALU.mult)
                    own.mark(ins)

            def add_squares_of(s, n, d, k):
                ve.wait_ge(ssq_ready, DC * (s["norm_i"] + 1) + d)
                if d == DC - 1:
                    ve.sem_inc(ssq_ready, 1)
                    return
                ve.wait_ge(xsq_ready, s["q0"] + d + 1)
                ve.tensor_tensor(ssq[:, 0:n], ssq[:, 0:n], work[:, k % 2, 0:n], ALU.add).then_inc(ssq_ready, 1)

            def norm(s, n):
                ve.wait_ge(norm_sd, s["norm_i"] + 1)
                ve.reciprocal(rstd[:, 0:n // P], std[:, 0:n // P]).then_inc(norm_rs, 1)
                ve.wait_ge(norm_pe, 2 * s["norm_i"] + 2)

            def zero_ssq():
                step(ve.memset(ssq[:, :], 0.0))

            def set_gate(s, scale=None):
                m = s["mod"] + 2
                for h in range(2):
                    if scale is None:
                        ins = ve.tensor_scalar(gate[:, :, h], mods[:, m, :, h], 0.5 if s["kind"] == "ffn" else 1.0,
                                               None, ALU.mult)
                    else:
                        ins = ve.tensor_tensor(gate[:, :, h], mods[:, m, :, h], scale, ALU.mult)
                step(ins)

            def normed(n, d, factor):
                for h, cols in halves(n):
                    ins = ve.scalar_tensor_tensor(work[:, d % 2, cols], X[:, d, cols], factor(d, h),
                                                  PS[:, BC_BANK, cols], ALU.mult, ALU.mult)
                ins.then_inc(t_ready, 1)

            def h_chunks(s, n, t0, h0, shift, factor, lo=0, ds=range(DC)):
                if h0:
                    ve.wait_ge(h_ready, h0 + ds.start)
                normed(n, ds.start, factor)
                for d in ds:
                    if d + 1 < ds.stop:
                        if h0 + d:
                            ve.wait_ge(h_ready, h0 + d)
                        normed(n, d + 1, factor)
                    ve.wait_ge(h_hi_ready, t0 + d + 1)
                    for h, cols in halves(n):
                        to = slice(lo + cols.start, lo + cols.stop)
                        high = H_hi[:, d, to].bitcast(F32)
                        if shift is None:
                            ins = ve.tensor_tensor(H_lo[:, d, to], work[:, d % 2, cols], high, ALU.subtract)
                        else:
                            ins = ve.scalar_tensor_tensor(H_lo[:, d, to], work[:, d % 2, cols],
                                                          mods[:, shift, d, h:h + 1], high, ALU.add, ALU.subtract)
                    ins.then_inc(h_ready, 1)
                if s is not stages[0] and not lo:
                    zero_ssq()

            def residual(s, n, c, bank, d, u, squares=True):
                if u is not None:
                    ve.wait_ge(unit_done, u + (RING + 1))
                for h, cols in halves(n):
                    if s.get("mod") is None:
                        ins = ve.tensor_tensor(X[:, d, cols], PS[:, bank, cols], X[:, d, cols], ALU.add)
                    else:
                        ins = ve.scalar_tensor_tensor(X[:, d, cols], PS[:, bank, cols], gate[:, d, h:h + 1],
                                                      X[:, d, cols], ALU.mult, ALU.add)
                ins.then_inc(psum_free, 1)
                if squares:
                    ve.wait_ge(psum_free, c + (RING + 1))
                    add_square(DC * (s["norm_i"] + 1) + d, d, n)

            def linear_out(s, u_off, c_off, n):
                def body(i):
                    for k in range(4):
                        residual(s, n, s["c0"] + c_off + 4 * i + k, (s["c0"] + c_off + k) % RING,
                                 4 * i + k, s["u0"] + u_off + 4 * i + k, False)
                        split(s["u0"] + AHEAD + u_off, i, 4, k)
                        add_squares_of(s, n, 4 * i + k, k)
                body(0)
                body(1)

            ve.memset(ones[:, :], 1.0)
            ve.memset(ssq[:, :], 0.0)
            ve.memset(silu_c[:, :, :], 0.0).then_inc(start_ready, 1)
            ve.wait_ge(in_vec, 16)
            ve.scalar_tensor_tensor(sp_t[:, 0, :], V("lam"), -1.0, V("lam"), ALU.mult, ALU.max)
            dl = V("diff_lam").rearrange("p (a b d) -> p a b d", a=2, b=2)
            step(ve.tensor_tensor(dots[:, :, :], dl[:, :, 0, :], dl[:, :, 1, :], ALU.mult))
            ve.tensor_reduce(lam[:, 0:2], dots[:, :, :], AX.X, ALU.add)\
              .then_inc(start_ready, 1)
            ve.wait_ge(in_pos, 32)
            step(ve.tensor_copy(posf[:, :], pos[:, :]))
            ang, r, cr = trig[:, 0, :, :], trig[:, 1, :, :], trig[:, 2, :, :]
            for t in range(TT):
                ins = ve.tensor_scalar(trig[:, 0, t, :], inv_freq[:, :], posf[:, t:t + 1], None, ALU.mult)
            step(ins)
            magic = 1.5 * 2.0 ** 23
            step(ve.tensor_scalar(cr, ang, 1.0 / (2 * math.pi), magic, ALU.mult, ALU.add))
            step(ve.tensor_scalar(cr, cr, magic, None, ALU.subtract))
            left = 2 * math.pi
            for n_bits in (6, 17, 30):
                part = math.floor(left * 2.0 ** n_bits) / 2.0 ** n_bits
                left -= part
                step(ve.scalar_tensor_tensor(r if n_bits == 30 else ang, cr, -part, ang, ALU.mult, ALU.add))
            step(ve.tensor_scalar(r, r, 3.1415925, -3.1415925, ALU.min, ALU.max))
            step(ve.scalar_tensor_tensor(cr, r, -1.0, r, ALU.mult, ALU.max))
            ve.tensor_scalar(cr, cr, -1.0, math.pi / 2, ALU.mult, ALU.add).then_inc(start_ready, 1)
            ve.wait_ge(start_act, 1)
            e, w, w2, acc = (sp_t[:, k, :] for k in (1, 2, 3, 0))
            step(ve.tensor_scalar(w, e, 2.0, None, ALU.add))
            step(ve.reciprocal(w, w))
            step(ve.tensor_tensor(w, w, e, ALU.mult))
            step(ve.tensor_tensor(w2, w, w, ALU.mult))
            step(ve.tensor_scalar(acc, w2, 1.0 / 17, None, ALU.mult))
            for k in range(15, 1, -2):
                step(ve.scalar_tensor_tensor(acc, acc, 1.0 / k, w2, ALU.add, ALU.mult))
            step(ve.scalar_tensor_tensor(w, acc, 1.0, w, ALU.add, ALU.mult))
            step(ve.tensor_scalar(w2, V("lam"), -8.0, 0.0, ALU.mult, ALU.max))
            step(ve.scalar_tensor_tensor(sp8[:, :], w, 16.0, w2, ALU.mult, ALU.add))
            step(ve.tensor_tensor(lam[:, 0:1], lam[:, 3:4], lam[:, 2:3], ALU.subtract))
            ve.tensor_scalar(lam[:, 0:1], lam[:, 0:1], LAM_INIT, None, ALU.subtract)
            ve.wait_ge(start_act, 2)
            for h in range(2):
                ve.tensor_copy(b_cos[:, :, 16 * h:16 * h + 16], trig[:, 4, :, :])
                ins = ve.tensor_scalar(b_sin[:, :, 16 * h:16 * h + 16], trig[:, 3, :, :], -1.0 if h == 0 else 1.0,
                                       None, ALU.mult)
            step(ins)
            ve.wait_ge(in_x, 16)
            for d in range(DC):
                add_square(d, d, 2 * T)
            norm(stages[0], 2 * T)
            zero_ssq()
            take_mod(0)
            for k in range(AHEAD):
                split(0, 0, 4, k)
            take_mod(1)
            gains(stages[0])
            own.sync()

            tp = its = regions = 0
            for s in stages:
                n, last = s["n"], s is stages[-1]
                factor = (lambda d, h: gain[:, d, h:h + 1]) if s.get("mod") is not None else \
                    (lambda d, h: V(s["gain"])[:, d:d + 1])
                if s["kind"] in ("pool", "diff", "dil"):
                    ve.sem_inc(region_free, 1)
                if s is not stages[0]:
                    gains(s)
                    norm(s, n)

                if s["kind"] == "ffn":
                    h_chunks(s, n, s["t0"], s["h0"], s["mod"], factor)

                    def pair(i, k):
                        ve.wait_ge(silu_ready, s["f0"] + 2 * i + (k + 1))
                        ve.wait_ge(unit_done, RING + s["u0"] + 4 * i + (2 * k + 2))
                        m = work[:, 2, 0:n]
                        ve.wait_ge(gu_ready, s["f0"] + 2 * i + (k + 1))
                        ve.tensor_tensor(m, work[:, k, 0:n], PS[:, (s["c0"] + 2 * k + 1) % RING, 0:n], ALU.mult)\
                          .then_inc(psum_free, 2)
                        ve.wait_ge(psum_free, RING + s["c0"] + 4 * i + (2 * k + 2))
                        step(ve.tensor_copy(G_hi[:, 2 * i + k, 0:n], m))
                        ve.tensor_tensor(G_lo[:, 2 * i + k, 0:n], m, G_hi[:, 2 * i + k, 0:n], ALU.subtract)\
                          .then_inc(gu_ready, 1)

                    def body(i, with_ada=False):
                        for k in range(4):
                            split(s["u0"] + AHEAD, i, 4, k)
                            if k % 2:
                                pair(i, k // 2)
                        if with_ada:
                            take_mod(s["ada"][0] + i)
                    n_ada = s["ada"][1] - s["ada"][0] if s["ada"] else 0
                    if n_ada:
                        own.loop(0, n_ada, 4, lambda i: body(i, True))
                    if n_ada < FC // 2:
                        own.loop(n_ada, FC // 2, 2, body)
                    own.sync()
                    if s["mod"] is not None:
                        set_gate(s)

                    def body(i):
                        for k in range(4):
                            for part in range(3):
                                split(s["u0"] + 2 * FC + AHEAD, i, 12, 3 * k + part)
                            c1 = s["c0"] + 2 * FC
                            residual(s, n, c1 + 4 * i + k, (c1 + k) % RING, 4 * i + k,
                                     s["u0"] + 2 * FC + 12 * i + 3 * k + 2, not last)
                    body(0)
                    body(1)

                elif s["kind"] == "pool":
                    h_chunks(s, n, s["t0"], s["h0"], s["mod"], factor)
                    set_gate(s, V("pool_scale"))
                    for g in range(4):
                        ve.wait_ge(mix_hi_ready, g + 1)
                        ve.tensor_tensor(mix_lo[:, g, :, :], mix[:, g, :, :], mix_hi[:, g, :, :], ALU.subtract)\
                          .then_inc(mix_ready, 1)
                    for half in range(2):
                        for t in range(4):
                            w = slice(half * 512, half * 512 + 512)
                            ve.wait_ge(z_hi_ready, 4 * half + t + 1)
                            ve.tensor_tensor(z_lo[:, t, w], PS[:, t + 4 * half, :], z_hi[:, t, w], ALU.subtract)\
                              .then_inc(z_ready, 1)
                    for d in range(DC + 1):
                        if d in (2, 4):
                            split(s["u0"] + AHEAD, 0, 4, d // 2 - 1)
                        if d < DC:
                            ve.wait_ge(mix_done, d + 1)
                            residual(s, n, s["c0"] + d, (s["c0"] + d) % RING, d, None, False)
                        if d:
                            add_squares_of(s, n, d - 1, d - 1)

                elif s["kind"] == "diff":
                    h_chunks(s, n, s["t0"], s["h0"], s["mod"], factor)
                    ve.wait_ge(stage_ld, 64)
                    ve.tensor_scalar(d_g[:, :], d_g[:, :], 1.0 - LAM_INIT, None, ALU.mult)
                    set_gate(s)

                    def rope(bank, dst, t):
                        src = PS[:, bank, :].rearrange("p (x c) -> p x c", c=64)
                        o0 = work[:, 0, :].rearrange("p (x c) -> p x c", c=64)
                        ve.tensor_tensor(o0, src, d_cos[:, t, :].unsqueeze(1).to_broadcast([P, 8, 64]), ALU.mult)
                        for half in range(2):
                            o1 = work[:, 1, :].rearrange("p (x a c) -> p x a c", a=2, c=32)[:, :, :, 16 * half:16 * half + 16]
                            other = PS[:, bank, :].rearrange("p (x a c) -> p x a c", a=2, c=32)[:, :, :, 16 - 16 * half:32 - 16 * half]
                            sn = d_sin[:, t, :].rearrange("p (a c) -> p a c", c=32)[:, :, 16 * half:16 * half + 16]
                            ins = ve.tensor_tensor(o1, other, sn.unsqueeze(1).to_broadcast([P, 8, 2, 16]), ALU.mult)
                        step(ins)
                        return ve.tensor_tensor(dst, work[:, 0, :], work[:, 1, :], ALU.add)

                    for g in range(6):
                        for q in range(4):
                            split(s["u0"] + AHEAD, 0, 4, 4 * g + q)
                        ve.wait_ge(unit_done, RING + s["u0"] + 4 * g + 4)
                        cols = slice((g % 2) * 512, (g % 2) * 512 + 512)
                        bank = 4 * (g % 2)
                        dst = (d_KN, d_VN, d_QN)[g // 2]
                        plain = {0: (2, 3), 1: (0, 1, 2, 3), 2: ()}[g // 2]
                        for t in plain:
                            ins = ve.tensor_copy(dst[:, t, cols], PS[:, bank + t, :])
                        if g // 2 != 1:
                            for t in range(TT):
                                ins = rope(bank + t, dst[:, t, cols], t)
                                if t < TT - 1:
                                    step(ins)
                        ins.then_inc(kn_ready, 1)
                        ve.wait_ge(kn_ready, g + 1)
                        ve.sem_inc(proj_taken, 1)

                    tp += HEADS + HEADS // 2

                    def maxima(it):
                        at = 2 * (it % 2)
                        ve.wait_ge(s_done, its + it + 1)
                        step(ve.tensor_reduce(stat[:, at:at + 2], PS[:, at:at + 2, :], AX.X, ALU.max))
                        ve.tensor_scalar(stat[:, 4 + at:6 + at], stat[:, at:at + 2], -DIFF_SCALE, None, ALU.mult)\
                          .then_inc(nb_ready, 1)

                    def weights(it):
                        at = 2 * (it % 2)
                        ve.wait_ge(p_ready, its + it + 1)
                        step(ve.reciprocal(stat[:, 12 + at:14 + at], stat[:, 8 + at:10 + at]))
                        step(ve.tensor_scalar(d_P[:, it % 2, 1, :], d_P[:, it % 2, 1, :], stat[:, 13 + at:14 + at],
                                              lam[:, 0:1], ALU.mult, ALU.mult))
                        if it >= 2:
                            ve.wait_ge(tp_done, tp + it - 1)
                        ve.scalar_tensor_tensor(d_A[:, it % 2, :], d_P[:, it % 2, 0, :], stat[:, 12 + at:13 + at],
                                                d_P[:, it % 2, 1, :], ALU.mult, ALU.add).then_inc(a_ready, 1)

                    maxima(0)
                    for it in range(2 * HEADS):
                        if it + 1 < 2 * HEADS:
                            maxima(it + 1)
                        weights(it)
                    tp += 2 * HEADS
                    its += 2 * HEADS
                    ve.wait_ge(o_sd, 1)
                    step(ve.reciprocal(stat[:, 48:64], stat[:, 32:48]))
                    for hh in range(HEADS // 2 + 1):
                        if hh < HEADS // 2:
                            for it in range(4 * hh, 4 * hh + 4):
                                h, qt = divmod(it, TT)
                                o = d_ON[:, qt, h * P:(h + 1) * P]
                                ins = ve.scalar_tensor_tensor(o, o, stat[:, 48 + it:49 + it], d_g[:, :], ALU.mult, ALU.mult)
                            ins.then_inc(on_ready, 1)
                        if hh == 0:
                            continue
                        hh = hh - 1
                        ve.wait_ge(oh_hi, hh + 1)
                        ve.tensor_tensor(H_lo[:, 2 * hh:2 * hh + 2, 0:T],
                                         PS[:, 4 + hh, :].rearrange("p (h t) -> p h t", h=2),
                                         H_hi[:, 2 * hh:2 * hh + 2, 0:T], ALU.subtract).then_inc(oh_ready, 2)
                    linear_out(s, 24, 0, T)

                elif s["kind"] == "final":
                    zero_ssq()
                    for d in range(DC + 1):
                        if d < DC:
                            ve.scalar_tensor_tensor(X[:, d, 0:T], X[:, d, 0:T], V("final_g")[:, d:d + 1],
                                                    PS[:, BC_BANK, 0:T], ALU.mult, ALU.mult).then_inc(xs_ready, 1)
                        if d:
                            add_squares_of(s, T, d - 1, d - 1)

                elif s["kind"] == "lru":
                    ve.memset(l_XB[:, :, 0:3], 0.0)
                    h_chunks(s, n, s["t0"], s["h0"], None, lambda d, h: V("a_norm")[:, d:d + 1])
                    for k in range(16):
                        split(s["u0"] + AHEAD, 0, 4, k)
                        d = k // 2
                        c = s["c0"] + k
                        if k % 2:
                            ve.wait_ge(xc_hi, d + 1)
                            ve.tensor_tensor(H_lo[:, d, T:2 * T], l_XC[:, d, :], H_hi[:, d, T:2 * T], ALU.subtract)\
                              .then_inc(xc_lo, 1)
                            ve.wait_ge(gelu_done, d + 1)
                            ve.sem_inc(psum_free, 1)
                            continue
                        ve.wait_ge(unit_done, RING + s["u0"] + k + 1)
                        ve.tensor_copy(l_XB[:, d, 3:T + 3], PS[:, c % RING, 0:T]).then_inc(psum_free, 1)
                        ve.wait_ge(psum_free, RING + c + 1)
                        cw = V("conv_w").rearrange("p (k d) -> p k d", k=4)
                        step(ve.tensor_scalar(l_XC[:, d, :], l_XB[:, d, 0:T], cw[:, 0, d:d + 1],
                                              V("conv_b")[:, d:d + 1], ALU.mult, ALU.add))
                        for j in range(1, 4):
                            ins = ve.scalar_tensor_tensor(l_XC[:, d, :], l_XB[:, d, j:j + T], cw[:, j, d:d + 1],
                                                          l_XC[:, d, :], ALU.mult, ALU.add)
                            if j < 3:
                                step(ins)
                        ins.then_inc(xc_ready, 1)
                    for half in range(2):
                        split(s["u0"] + AHEAD, 0, 4, 16 + half)
                    for q in range(4):
                        two = slice(2 * q, 2 * q + 2)
                        ve.wait_ge(sig_done, 2 * q + 2)
                        ve.tensor_tensor(l_H[:, two, :], l_R[:, two, :], sp8[:, two].unsqueeze(2).to_broadcast([P, 2, T]),
                                         ALU.mult).then_inc(yr_ready, 1)
                    for q in range(4):
                        two = slice(2 * q, 2 * q + 2)
                        ve.wait_ge(sig_done, DC + 2 * q + 2)
                        own.mark(ve.tensor_tensor(l_I[:, two, :], l_I[:, two, :], l_XC[:, two, :], ALU.mult))
                    for q in range(4):
                        two = slice(2 * q, 2 * q + 2)
                        ve.wait_ge(a_t_done, q + 1)
                        step(ve.tensor_tensor(l_H[:, two, :], l_A[:, two, :], l_A[:, two, :], ALU.mult))
                        ve.scalar_tensor_tensor(l_T[:, two, :], l_H[:, two, :], 1.0, l_T[:, two, :], ALU.add, ALU.mult)\
                          .then_inc(om_ready, 1)
                    for q in range(4):
                        two = slice(2 * q, 2 * q + 2)
                        ve.wait_ge(sqrt_done, q + 1)
                        step(ve.tensor_tensor(l_T[:, two, :], l_T[:, two, :], l_I[:, two, :], ALU.mult))
                        for d in (2 * q, 2 * q + 1):
                            ins = ve.tensor_tensor_scan(l_H[:, d, :], l_A[:, d, :], l_T[:, d, :], 0.0, ALU.mult, ALU.add)
                        step(ins)
                        ve.tensor_tensor(l_H[:, two, :], l_H[:, two, :], l_G[:, two, :], ALU.mult).then_inc(y_ready, 1)
                    for q in range(4):
                        two = slice(2 * q, 2 * q + 2)
                        ve.wait_ge(y_hi, q + 1)
                        ve.tensor_tensor(H_lo[:, two, 0:T], l_H[:, two, :], H_hi[:, two, 0:T], ALU.subtract)\
                          .then_inc(y_lo, 2)
                    linear_out(s, 18, 16, T)

                elif s["kind"] == "dil":
                    h_chunks(s, n, s["t0"], s["h0"], None, lambda d, h: V("kv_norm")[:, d:d + 1])
                    ve.wait_ge(stage_ld, 16 * 7)
                    for g in range(9):
                        split_units(s, 4 * g, 4)
                        if g < 3:
                            if g:
                                ve.wait_ge(ss_ready, g)
                            h_chunks(s, n, s["t0"] + DC, s["h0"] + DC, None, lambda d, h: V("b_norm")[:, d:d + 1], T,
                                     H_PARTS[g])
                        heads = 2 if g < 3 else 4
                        w = heads * P
                        bank = 2 * (g % 2)
                        ve.wait_ge(sq_done, g + 1)
                        ve.tensor_reduce(stat[:, 0:TT * heads],
                                         work[:, 0:TT, 0:w].rearrange("p t (h c) -> p t h c", c=P), AX.X, ALU.add)\
                          .then_inc(ss_ready, 1)
                        ve.wait_ge(sd_done, g + 1)
                        step(ve.reciprocal(stat[:, 16:16 + TT * heads], stat[:, 8:8 + TT * heads]))
                        if g >= 2:
                            ve.wait_ge(tp_done, tp + (g - 1 if g < 5 else 3 + 2 * (g - 4)))
                        table = b_gk[:, g, :] if g < 3 else b_gq[:, (g - 3) // 2, :]
                        for t in range(TT):
                            for h in range(heads):
                                at = 16 + t * heads + h
                                ins = ve.scalar_tensor_tensor(b_N[:, g % 2, t, h * P:(h + 1) * P],
                                                              PS[:, bank + t, h * P:(h + 1) * P], stat[:, at:at + 1],
                                                              table, ALU.mult, ALU.mult)
                        if g < 3:
                            ins = ve.tensor_copy(b_VN[:, :, g, :], PS[:, bank:bank + 2, w:2 * w])
                        step(ins)
                        ve.sem_inc(proj_taken, 1)
                        y = b_N[:, g % 2, :, 0:w].rearrange("p t (h c) -> p t h c", c=P)
                        ve.wait_ge(kn_ready, 6 + g)
                        for half in range(2):
                            sn = b_sin[:, :, 16 * half:16 * half + 16].unsqueeze(2).to_broadcast([P, TT, heads, 16])
                            ve.tensor_tensor(b_rb[:, :, 0:heads, 16 * half:16 * half + 16],
                                             y[:, :, :, 16 - 16 * half:32 - 16 * half], sn, ALU.mult)
                        step(ve.tensor_tensor(b_ra[:, :, 0:heads, :], y[:, :, :, 0:32],
                                              b_cos[:, :, :].unsqueeze(2).to_broadcast([P, TT, heads, 32]), ALU.mult))
                        ve.tensor_tensor(y[:, :, :, 0:32], b_ra[:, :, 0:heads, :], b_rb[:, :, 0:heads, :], ALU.add)\
                          .then_inc(kn_ready, 1)
                    tp += 15

                    def maxima(it):
                        qt, b = it % TT, it % 2
                        w = 3 * (qt + 1) * P
                        ve.wait_ge(s_done, its + it + 1)
                        if it >= 3:
                            ve.wait_ge(tp_done, tp + it - 2)
                        step(ve.scalar_tensor_tensor(b_S[:, it % 3, 0:w], PSf[:, b * 1024:b * 1024 + w], DIL_SCALE,
                                                     b_mask[:, qt, 0:w], ALU.mult, ALU.add))
                        step(ve.tensor_reduce(stat[:, 36 + b:37 + b], b_S[:, it % 3, 0:w], AX.X, ALU.max))
                        ve.tensor_scalar(stat[:, 32 + b:33 + b], stat[:, 36 + b:37 + b], -1.0, None, ALU.mult)\
                          .then_inc(nb_ready, 1)

                    def weights(it):
                        b = it % 2
                        w = 3 * (it % TT + 1) * P
                        ve.wait_ge(p_ready, its + it + 1)
                        step(ve.reciprocal(stat[:, 38 + b:39 + b], stat[:, 34 + b:35 + b]))
                        ve.tensor_scalar(b_S[:, it % 3, 0:w], b_S[:, it % 3, 0:w], stat[:, 38 + b:39 + b], None, ALU.mult)\
                          .then_inc(a_ready, 1)

                    def low_o(it):
                        h, qt = divmod(it, TT)
                        rows = slice(qt * P, (qt + 1) * P)
                        ve.wait_ge(o_hi, it + 1)
                        ve.tensor_tensor(H_lo[:, h, rows], PSf[:, (it % 2) * 1024 + 2944:(it % 2) * 1024 + 3072],
                                         H_hi[:, h, rows], ALU.subtract).then_inc(o_taken, 1)

                    maxima(0)
                    for it in range(2 * HEADS):
                        if it + 1 < 2 * HEADS:
                            maxima(it + 1)
                        if it >= 2:
                            low_o(it - 2)
                        weights(it)
                    low_o(2 * HEADS - 2)
                    low_o(2 * HEADS - 1)
                    tp += 2 * HEADS
                    its += 2 * HEADS
                    linear_out(s, 36, 0, T)


def chunks(w):
    k, m = w.shape[0] // P, w.shape[1] // P
    return w.reshape(k, P, m, P).transpose(2, 1, 0, 3).reshape(m, P, k * P)


def wide(w):
    n = w.shape[1] // 512
    return w.reshape(4, 2, P, n, 512).transpose(3, 0, 2, 1, 4).reshape(4 * n, P, 1024)


def ffn_units(w_in, w_out):
    g_u = chunks(w_in).reshape(2, FC, P, D).transpose(1, 0, 2, 3).reshape(2 * FC, P, D)
    w = w_out.reshape(FC, P, DC, P).transpose(2, 1, 0, 3)
    outs = np.zeros((DC, 3, P, D), w_out.dtype)
    at = 0
    for part, blocks in enumerate(W_OUT_PARTS):
        outs[:, part, :, 0:blocks * P] = w[:, :, at:at + blocks].reshape(DC, P, blocks * P)
        at += blocks
    return [g_u, outs.reshape(3 * DC, P, D)]


def column(v):
    return v.reshape(-1, P).T


def constants():
    n = np.arange(T)
    mix = np.zeros((4, T, T), np.float64)
    for g, win in enumerate((2, 4, 8, 16)):
        lo = np.clip(n - win // 2, 0, T - 1)
        hi = np.clip(n - win // 2 + win - 1, 0, T - 1)
        mix[g] = ((n[:, None] >= lo) & (n[:, None] <= hi)) / (hi - lo + 1) - np.eye(T)
    mix = np.ascontiguousarray(mix.astype(np.float32).reshape(4, TT, P, T).transpose(2, 0, 1, 3))
    inv = (np.float32(10000.0) ** (-np.arange(0, 32, 2, dtype=np.float32) / np.float32(32))).astype(np.float32)
    ang = np.stack([(n // 64).astype(np.float32)[:, None] * inv, (n % 64).astype(np.float32)[:, None] * inv], 1)
    cos = np.concatenate([np.cos(ang), np.cos(ang)], -1).reshape(T, 64)
    sin = np.concatenate([-np.sin(ang), np.sin(ang)], -1).reshape(T, 64)
    q, k = n[:, None], n[None, :]
    allowed = [(q >= k) & ((q - k) % d == 0) & ((q - k) // d <= P) for d in (1, 4, 16)]
    mask = np.full((P, TT, 768), NEG, np.float32)
    for t in range(TT):
        w = (t + 1) * P
        for g in range(3):
            mask[:, t, g * w:(g + 1) * w] = np.where(allowed[g][t * P:(t + 1) * P, 0:w], 0.0, NEG)
    inv2 = (np.float32(500000.0) ** (-np.arange(0, 32, 2, dtype=np.float32) / np.float32(32))).astype(np.float32)
    tiles = lambda v: np.ascontiguousarray(v.astype(np.float32).reshape(TT, P, -1).transpose(1, 0, 2))
    return dict(ident=np.eye(P, dtype=np.float32), mix=mix,
                d_cos=tiles(cos), d_sin=tiles(sin), mask=mask,
                inv_freq=np.ascontiguousarray(np.broadcast_to(inv2, (P, 16))))


def lay_out(i):
    w = []
    fi, fo = i["ffn_w_in"], i["ffn_w_out"]
    w += ffn_units(fi[0, 0], fo[0, 0])
    w += [i["pool_w"][0].reshape(2, 4, P, 2 * P).transpose(0, 2, 1, 3).reshape(2, P, D)]
    w += ffn_units(fi[0, 1], fo[0, 1])
    w += ffn_units(fi[1, 0], fo[1, 0])
    qkv = i["diff_w_qkv"][0]
    w += [wide(qkv[:, D:2 * D]), wide(qkv[:, 2 * D:]), wide(qkv[:, 0:D]), chunks(i["diff_w_o"][0])]
    w += ffn_units(fi[1, 1], fo[1, 1])
    w += [chunks(i["a_w_in_2"][0]).reshape(2, DC, P, D)[::-1].transpose(1, 0, 2, 3).reshape(2 * DC, P, D)]
    w += [i[name][0].transpose(1, 0, 2).reshape(1, P, D) for name in ("a_gate_a_w_2", "a_gate_x_w_2")]
    w += [chunks(i["a_w_out_2"][0])]
    w += ffn_units(i["a_ffn_w_in_2"][0], i["a_ffn_w_out_2"][0])
    w += [wide(i["w_kv_2"]), wide(i["b_w_q_2"][0]), chunks(i["b_w_o_2"][0])]
    w += ffn_units(i["b_ffn_w_in_2"][0], i["b_ffn_w_out_2"][0])
    ada = i["ada_w"].reshape(2, DC, P, 9, DC, 4, 32).transpose(0, 3, 1, 2, 5, 4, 6)
    vecs = dict(
        c=np.stack([i["c"][0], i["c_ctx"]], -1).reshape(DC, P, 2).transpose(1, 0, 2).reshape(P, 16),
        ada_b=column(i["ada_b"]), norm_g=column(i["norm_g"]), pool_scale=column(i["pool_scale"]),
        final_g=column(i["final_g"]), a_norm=column(i["a_norm_2"]), conv_w=column(i["a_conv_w_2"]),
        conv_b=column(i["a_conv_b_2"]), ga_b=column(i["a_gate_a_b_2"]), gx_b=column(i["a_gate_x_b_2"]),
        lam=column(i["a_lambda_2"]), a_ffn=column(i["a_ffn_norm_2"]), kv_norm=column(i["kv_norm_2"]),
        b_norm=column(i["b_norm_2"]), b_ffn=column(i["b_ffn_norm_2"]),
        diff_lam=np.broadcast_to(i["diff_lam"].reshape(1, 256), (P, 256)))
    x = np.concatenate([i["x"][0], i["ctx"][0]], 0)
    spread = lambda v: np.ascontiguousarray(np.broadcast_to(v, (P,) + v.shape))
    arrays = dict(
        xT=np.ascontiguousarray(x.T.reshape(DC, P, 2 * T).transpose(1, 0, 2)),
        w=np.concatenate(w, 0), ada_w=np.ascontiguousarray(ada).reshape(N_MODS * DC, P, D),
        vec=np.ascontiguousarray(np.concatenate([vecs[name] for name in VEC], 1)),
        positions=np.ascontiguousarray(i["positions_2"][0].reshape(TT, P).T),
        subln_g=spread(i["diff_subln_g"][0]), k_norm=spread(i["k_norm_2"]), q_norm=spread(i["b_q_norm_2"][0]))
    arrays.update(constants())
    return arrays


def kernel(**inputs):
    import concourse.bacc as bacc
    from concourse.bass_utils import run_bass_kernel_spmd

    nc = bacc.Bacc("TRN2", target_bir_lowering=False, num_devices=1)
    arrays = lay_out({name: np.asarray(v) for name, v in inputs.items()})
    maps, aps = {}, {}
    for name, v in arrays.items():
        maps[f"in_{name}"] = v
        aps[name] = nc.dram_tensor(f"in_{name}", v.shape, mybir.dt.from_np(v.dtype), kind="ExternalInput").ap()
    out = nc.dram_tensor("out_x", (P, DC, T), F32, kind="ExternalOutput").ap()
    build(nc, aps, out)
    got = run_bass_kernel_spmd(nc, [maps], core_ids=[0]).results[0]["out_x"]
    return np.ascontiguousarray(got.transpose(2, 1, 0).reshape(1, T, D))
```
